# Optimizing a Trainium2 kernel written in Bass

```python
import math
import jax, jax.numpy as jnp
from jax import lax
import numpy as np

D_MODEL = 1024
BATCH = 1
SEQ = 256
DEPTH = 2

CHUNK = 64
HEAD_DIM = 64
ROT_DIM = HEAD_DIM // 4
ROPE_THETA = 500000.0
QBLOCK = 128
EPS = 1e-6
MIX_WIDTH = D_MODEL
FOX_HEADS = (MIX_WIDTH // 2) // HEAD_DIM
FOX_W = FOX_HEADS * HEAD_DIM
DIFF_HEADS = (MIX_WIDTH // 2) // (2 * HEAD_DIM)
DIFF_VDIM = 2 * HEAD_DIM
DIFF_QK = DIFF_HEADS * 2 * HEAD_DIM
DIFF_V = DIFF_HEADS * DIFF_VDIM
AB_SPLITS = [FOX_W, FOX_W, FOX_W, FOX_HEADS, DIFF_QK, DIFF_QK, DIFF_V]
AB_IN = sum(AB_SPLITS)
SWA_Q_HEADS = MIX_WIDTH // HEAD_DIM
SWA_KV_HEADS = 4
SWA_GROUP = SWA_Q_HEADS // SWA_KV_HEADS
WINDOW = 128
WINDOW_CHUNKS = WINDOW // CHUNK
C_IN = (SWA_Q_HEADS + 2 * SWA_KV_HEADS) * HEAD_DIM
PEER_HEADS = 8
PEER_KEYS = 128
PEER_EXPERTS = PEER_KEYS * PEER_KEYS
PEER_QDIM = 256
PEER_HALF = PEER_QDIM // 2
PEER_TOPK = 16
PEER_BLOCK = 128

kernel_name = 'hybrid_fox_diff_swa_peer_trunk'

def rmsnorm(x, g):
    xf = x.astype(jnp.float32)
    y = xf * lax.rsqrt(jnp.mean(xf * xf, axis=-1, keepdims=True) + EPS)
    return (y * g.astype(jnp.float32)).astype(x.dtype)

def rope_tables(seq):
    inv = 1.0 / (ROPE_THETA ** (jnp.arange(0, ROT_DIM, 2, dtype=jnp.float32) / ROT_DIM))
    ang = jnp.arange(seq, dtype=jnp.float32)[:, None] * inv[None, :]
    return jnp.cos(ang), jnp.sin(ang)

def apply_partial_rope(x, cos, sin):
    shape = (cos.shape[0],) + (1,) * (x.ndim - 3) + (cos.shape[1],)
    c = cos.reshape(shape).astype(x.dtype)
    s = sin.reshape(shape).astype(x.dtype)
    half = ROT_DIM // 2
    x1, x2, rest = x[..., :half], x[..., half:ROT_DIM], x[..., ROT_DIM:]
    return jnp.concatenate([x1 * c - x2 * s, x2 * c + x1 * s, rest], axis=-1)

def heads_first(t, n_heads):
    b, s = t.shape[0], t.shape[1]
    return t.reshape(b, s, n_heads, -1).transpose(0, 2, 1, 3)

def query_block_sweep(block_fn, seq):
    out = lax.map(block_fn, jnp.arange(seq // QBLOCK))
    nb, b, h, qb, dv = out.shape
    return out.transpose(1, 2, 0, 3, 4).reshape(b, h, nb * qb, dv)

def forgetting_attention(q, k, v, log_f):
    seq = q.shape[2]
    cum = jnp.cumsum(log_f, axis=-1)
    kpos = jnp.arange(seq)
    scale = HEAD_DIM ** -0.5

    def block(i):
        start = i * QBLOCK
        qb = lax.dynamic_slice_in_dim(q, start, QBLOCK, axis=2)
        cq = lax.dynamic_slice_in_dim(cum, start, QBLOCK, axis=2)
        qpos = start + jnp.arange(QBLOCK)
        logits = (jnp.einsum('bhqd,bhkd->bhqk', qb, k).astype(jnp.float32) * scale
                  + (cq[..., :, None] - cum[..., None, :]))
        logits = jnp.where(kpos[None, :] <= qpos[:, None], logits, -jnp.inf)
        p = jax.nn.softmax(logits, axis=-1)
        return jnp.einsum('bhqk,bhkd->bhqd', p.astype(v.dtype), v)

    return query_block_sweep(block, seq)

def differential_attention(q1, q2, k1, k2, v, lam):
    seq = q1.shape[2]
    kchunk = jnp.arange(seq) // CHUNK
    scale = HEAD_DIM ** -0.5

    def block(i):
        start = i * QBLOCK
        qa = lax.dynamic_slice_in_dim(q1, start, QBLOCK, axis=2)
        qb = lax.dynamic_slice_in_dim(q2, start, QBLOCK, axis=2)
        qchunk = (start + jnp.arange(QBLOCK)) // CHUNK
        mask = kchunk[None, :] <= qchunk[:, None]
        l1 = jnp.where(mask, jnp.einsum('bhqd,bhkd->bhqk', qa, k1).astype(jnp.float32) * scale, -jnp.inf)
        l2 = jnp.where(mask, jnp.einsum('bhqd,bhkd->bhqk', qb, k2).astype(jnp.float32) * scale, -jnp.inf)
        p = jax.nn.softmax(l1, axis=-1) - lam * jax.nn.softmax(l2, axis=-1)
        return jnp.einsum('bhqk,bhkd->bhqd', p.astype(v.dtype), v)

    return query_block_sweep(block, seq)

def sliding_window_sink_attention(q, k, v, sinks):
    b, seq = q.shape[0], q.shape[1]
    nc = seq // CHUNK
    qc = q.reshape(b, nc, CHUNK, SWA_KV_HEADS, SWA_GROUP, HEAD_DIM)

    def band(t):
        pad = jnp.zeros((b, (WINDOW_CHUNKS - 1) * CHUNK) + t.shape[2:], t.dtype)
        tp = jnp.concatenate([pad, t], axis=1).reshape((b, nc + WINDOW_CHUNKS - 1, CHUNK) + t.shape[2:])
        return jnp.concatenate([tp[:, w:w + nc] for w in range(WINDOW_CHUNKS)], axis=2)

    kb, vb = band(k), band(v)
    logits = jnp.einsum('bnqkgd,bnskd->bnkgqs', qc, kb).astype(jnp.float32) * (HEAD_DIM ** -0.5)
    key_chunk = jnp.arange(nc)[:, None] - (WINDOW_CHUNKS - 1) + jnp.arange(WINDOW)[None, :] // CHUNK
    valid = key_chunk >= 0
    logits = jnp.where(valid[None, :, None, None, None, :], logits, -jnp.inf)
    sink = jnp.broadcast_to(
        sinks.astype(jnp.float32).reshape(SWA_KV_HEADS, SWA_GROUP)[None, None, :, :, None, None],
        logits.shape[:-1] + (1,))
    p = jax.nn.softmax(jnp.concatenate([logits, sink], axis=-1), axis=-1)[..., :-1]
    out = jnp.einsum('bnkgqs,bnskd->bnqkgd', p.astype(v.dtype), vb)
    return out.reshape(b, seq, SWA_Q_HEADS * HEAD_DIM)

def mixer_fox_diff(h, w_in, f_bias, lam_vecs, subln_gain, w_out, lam_init, cos, sin):
    b, seq, _ = h.shape
    proj = h @ w_in
    offs = np.cumsum(AB_SPLITS)[:-1].tolist()
    qa, ka, va, fa, qd, kd, vd = jnp.split(proj, offs, axis=-1)
    log_f = jax.nn.log_sigmoid(fa.astype(jnp.float32) + f_bias.astype(jnp.float32)).transpose(0, 2, 1)
    out_a = forgetting_attention(heads_first(qa, FOX_HEADS), heads_first(ka, FOX_HEADS),
                                 heads_first(va, FOX_HEADS), log_f)
    out_a = out_a.transpose(0, 2, 1, 3).reshape(b, seq, FOX_W)
    qd = apply_partial_rope(qd.reshape(b, seq, DIFF_HEADS, 2, HEAD_DIM), cos, sin)
    kd = apply_partial_rope(kd.reshape(b, seq, DIFF_HEADS, 2, HEAD_DIM), cos, sin)
    lv = lam_vecs.astype(jnp.float32)
    lam = jnp.exp(jnp.sum(lv[0] * lv[1])) - jnp.exp(jnp.sum(lv[2] * lv[3])) + lam_init
    out_b = differential_attention(qd[:, :, :, 0].transpose(0, 2, 1, 3), qd[:, :, :, 1].transpose(0, 2, 1, 3),
                                   kd[:, :, :, 0].transpose(0, 2, 1, 3), kd[:, :, :, 1].transpose(0, 2, 1, 3),
                                   heads_first(vd, DIFF_HEADS), lam)
    out_b = rmsnorm(out_b, subln_gain) * (1.0 - lam_init)
    out_b = out_b.transpose(0, 2, 1, 3).reshape(b, seq, DIFF_V)
    return jnp.concatenate([out_a, out_b], axis=-1) @ w_out

def mixer_swa(h, w_in, sinks, w_out, cos, sin):
    b, seq, _ = h.shape
    proj = h @ w_in
    q, k, v = jnp.split(proj, [SWA_Q_HEADS * HEAD_DIM, (SWA_Q_HEADS + SWA_KV_HEADS) * HEAD_DIM], axis=-1)
    q = apply_partial_rope(q.reshape(b, seq, SWA_Q_HEADS, HEAD_DIM), cos, sin)
    k = apply_partial_rope(k.reshape(b, seq, SWA_KV_HEADS, HEAD_DIM), cos, sin)
    v = v.reshape(b, seq, SWA_KV_HEADS, HEAD_DIM)
    return sliding_window_sink_attention(q, k, v, sinks) @ w_out

def peer_ffn(h, w_q, sub_keys, u, v):
    b, seq, d = h.shape
    tokens = h.reshape((b * seq) // PEER_BLOCK, PEER_BLOCK, d)
    keys = sub_keys.astype(jnp.float32)

    def block(xb):
        q = (xb @ w_q).astype(jnp.float32).reshape(PEER_BLOCK, PEER_HEADS, 2, PEER_HALF)
        s = jnp.einsum('phcd,hckd->phck', q, keys)
        sv, si = lax.top_k(s, PEER_TOPK)
        cand = (sv[:, :, 0, :, None] + sv[:, :, 1, None, :]).reshape(PEER_BLOCK, PEER_HEADS, -1)
        cand_idx = (si[:, :, 0, :, None] * PEER_KEYS + si[:, :, 1, None, :]).reshape(PEER_BLOCK, PEER_HEADS, -1)
        top_s, top_pos = lax.top_k(cand, PEER_TOPK)
        experts = jnp.take_along_axis(cand_idx, top_pos, axis=-1)
        g = jax.nn.softmax(top_s, axis=-1)
        act = jax.nn.gelu(jnp.einsum('phkd,pd->phk', u[experts], xb).astype(jnp.float32))
        return jnp.einsum('phk,phkd->pd', (g * act).astype(v.dtype), v[experts])

    return lax.map(block, tokens).reshape(b, seq, d)

def setup_inputs(seed: int = 0) -> dict:
    key = jax.random.key(seed)
    ks = jax.random.split(key, 17)
    n_even, n_odd = (DEPTH + 1) // 2, DEPTH // 2
    f32 = jnp.float32
    nrm = lambda k, shape, scale: jax.random.normal(k, shape, f32) * scale
    return {
        'x': nrm(ks[0], (BATCH, SEQ, D_MODEL), 1.0),
        'norm_mix': 1.0 + nrm(ks[1], (DEPTH, D_MODEL), 0.02),
        'norm_ffn': 1.0 + nrm(ks[2], (DEPTH, D_MODEL), 0.02),
        'norm_final': 1.0 + nrm(ks[3], (D_MODEL,), 0.02),
        'ab_w_in': nrm(ks[4], (n_even, D_MODEL, AB_IN), D_MODEL ** -0.5),
        'ab_f_bias': 3.0 + nrm(ks[5], (n_even, FOX_HEADS), 0.5),
        'ab_lambda': nrm(ks[6], (n_even, 4, HEAD_DIM), 0.1),
        'ab_subln': 1.0 + nrm(ks[7], (n_even, DIFF_VDIM), 0.02),
        'ab_w_out': nrm(ks[8], (n_even, MIX_WIDTH, D_MODEL), MIX_WIDTH ** -0.5),
        'c_w_in': nrm(ks[9], (n_odd, D_MODEL, C_IN), D_MODEL ** -0.5),
        'c_sinks': nrm(ks[10], (n_odd, SWA_Q_HEADS), 0.5),
        'c_w_out': nrm(ks[11], (n_odd, MIX_WIDTH, D_MODEL), MIX_WIDTH ** -0.5),
        'peer_w_q': nrm(ks[12], (DEPTH, D_MODEL, PEER_HEADS * PEER_QDIM), D_MODEL ** -0.5),
        'peer_sub_keys': nrm(ks[13], (DEPTH, PEER_HEADS, 2, PEER_KEYS, PEER_HALF), PEER_HALF ** -0.5),
        'peer_u': nrm(ks[14], (DEPTH, PEER_EXPERTS, D_MODEL), D_MODEL ** -0.5),
        'peer_v': nrm(ks[15], (DEPTH, PEER_EXPERTS, D_MODEL), PEER_HEADS ** -0.5),
    }

def reference(x, norm_mix, norm_ffn, norm_final, ab_w_in, ab_f_bias, ab_lambda, ab_subln, ab_w_out,
              c_w_in, c_sinks, c_w_out, peer_w_q, peer_sub_keys, peer_u, peer_v):
    cos, sin = rope_tables(x.shape[1])
    for l in range(DEPTH):
        h = rmsnorm(x, norm_mix[l])
        j = l // 2
        if l % 2 == 0:
            lam_init = 0.8 - 0.6 * math.exp(-0.3 * l)
            x = x + mixer_fox_diff(h, ab_w_in[j], ab_f_bias[j], ab_lambda[j], ab_subln[j], ab_w_out[j],
                                   lam_init, cos, sin)
        else:
            x = x + mixer_swa(h, c_w_in[j], c_sinks[j], c_w_out[j], cos, sin)
        h = rmsnorm(x, norm_ffn[l])
        x = x + peer_ffn(h, peer_w_q[l], peer_sub_keys[l], peer_u[l], peer_v[l])
    return rmsnorm(x, norm_final)


_drawn_inputs = setup_inputs


def setup_inputs(seed=0):
    import zlib

    import numpy as np

    out = dict(_drawn_inputs(seed))
    spreads = {}
    factors = {'norm_final': 2.98, 'c_sinks': 8.0}
    for name, (base, spread) in spreads.items():
        noise = np.random.default_rng([zlib.crc32(name.encode()), seed]).standard_normal(out[name].shape)
        drawn = base * np.exp(spread * noise) if base else spread * noise
        out[name] = __import__('jax').numpy.asarray(drawn.astype(out[name].dtype))
    for name, factor in factors.items():
        out[name] = (out[name] * factor).astype(out[name].dtype)
    return out
```

```python
from contextlib import ExitStack

import concourse.bass as bass
import numpy as np
from concourse import mybir

F32 = mybir.dt.float32
F32R = mybir.dt.float32r
BF16 = mybir.dt.bfloat16
U32 = mybir.dt.uint32
ALU = mybir.AluOpType
ACT = mybir.ActivationFunctionType
AX_X = mybir.AxisListType.X

P = 128
D = 1024
C = D // P
T = 256
TT = T // P
DEPTH = 2
CHUNK = 64
HD = 64
ROT = HD // 4
THETA = 500000.0
EPS = 1e-6
FOX_HEADS = 8
DIFF_HEADS = 4
LAM_INIT = 0.2
SWA_HEADS = 16
PEER_HEADS = 8
HC = 2 * PEER_HEADS
KEYS = 128
TOPK = 16
NEG = -1e30
REPLACED = -3e38

AB_BLOCKS, C_BLOCKS, OUT_BLOCKS, PQ_BLOCKS = 24, 12, 8, HC
SEGMENTS = [("in", AB_BLOCKS), ("out", OUT_BLOCKS), ("pq", PQ_BLOCKS), ("u", KEYS), ("v", KEYS)]
START = {}
_at = 0
for _l in range(DEPTH):
    for _name, _count in SEGMENTS:
        START[_name, _l] = _at
        _at += (C_BLOCKS if _l else AB_BLOCKS) if _name == "in" else _count
CHUNKS = _at
RAW = 4
AHEAD = 2
HALF = KEYS // 2
TOK = 4
TURNS = HALF // RAW

CF = {}
_at = 0
for _name, _count in [("ident", P), ("iota", P), ("cos", TT * ROT // 2), ("sin", TT * ROT // 2),
                      ("mv_scale", 1), ("mv_add", 1), ("st_scale", FOX_HEADS), ("st_add", FOX_HEADS)]:
    CF[_name] = slice(_at, _at + _count)
    _at += _count
CF_COLS = _at
CB = {}
_at = 0
for _name, _count in [("ident", P), ("fox0", P), ("fox1", T), ("chunk0", P), ("chunk1", T), ("swa1", T)]:
    CB[_name] = slice(_at, _at + _count)
    _at += _count
CB_COLS = _at


def float_constants():
    c = np.zeros((P, CF_COLS), np.float32)
    c[:, CF["ident"]] = np.eye(P)
    c[:, CF["iota"]] = np.arange(P)
    inv = (1.0 / (np.float32(THETA) ** (np.arange(0, ROT, 2, dtype=np.float32) / np.float32(ROT)))).astype(np.float32)
    angle = (np.arange(T, dtype=np.float32)[:, None] * inv[None, :]).astype(np.float32)
    for name, f in (("cos", np.cos), ("sin", np.sin)):
        c[:, CF[name]] = f(angle).astype(np.float32).reshape(TT, P, ROT // 2).transpose(1, 0, 2).reshape(P, -1)
    c[0:8, CF["mv_scale"]] = -8.0
    c[32:40, CF["mv_add"]] = 1.0
    for h in range(FOX_HEADS):
        c[h, CF["st_add"].start + h] = 1.0
        c[32 + h, CF["st_scale"].start + h] = 8.0
    return c


def mask_constants():
    c = np.zeros((P, CB_COLS), np.float32)
    q, k = np.arange(P)[:, None], np.arange(T)[None, :]
    c[:, CB["ident"]] = np.eye(P)
    c[:, CB["fox0"]] = np.where(k[:, :P] <= q, 0, NEG)
    c[:, CB["fox1"]] = np.where(k <= q + P, 0, NEG)
    c[:, CB["chunk0"]] = np.where(k[:, :P] // CHUNK <= q // CHUNK, 0, NEG)
    c[:, CB["chunk1"]] = np.where(k // CHUNK <= (q + P) // CHUNK, 0, NEG)
    away = (q + P) // CHUNK - k // CHUNK
    c[:, CB["swa1"]] = np.where((away >= 0) & (away <= 1), 0, NEG)
    return c


def attention_units(l):
    if l == 0:
        out = [("fox", 0, range(4)), ("fox", 0, range(4, 8))]
        out += [("fox", 1, range(h, h + 2)) for h in range(0, 8, 2)]
        out += [("diff", 0, range(h, h + 2)) for h in (0, 2)]
        out += [("diff", 1, range(h, h + 1)) for h in range(DIFF_HEADS)]
        return out
    out = [("swa", 0, range(h, h + 4)) for h in range(0, SWA_HEADS, 4)]
    return out + [("swa", 1, range(h, h + 2)) for h in range(0, SWA_HEADS, 2)]


UNITS = [attention_units(0), attention_units(1)]


def trunk(nc, x, gains, gain_final, consts, masks, w_ab, w_f, f_bias, lam_vecs, subln, w_ab_out, w_c, sinks,
          w_c_out, w_pq, keys_t, u_t, v_e, out):
    with ExitStack() as ctx:
        def sb(name, shape, dt=F32):
            return ctx.enter_context(nc.sbuf_tensor(name, shape, dt))

        def psum(name, shape, dt=F32):
            return ctx.enter_context(nc.psum_tensor(name, shape, dt))

        def sem(name):
            return ctx.enter_context(nc.semaphore(name))

        xs = sb("xs", [P, TT, D])
        act = sb("act", [P, KEYS * T])
        h_hi = sb("h_hi", [P, C, T], F32R)
        h_lo = sb("h_lo", [P, C, T], F32R)
        raw = sb("raw", [P, RAW, D])
        w_hi = sb("w_hi", [P, AHEAD, D], F32R)
        w_lo = sb("w_lo", [P, AHEAD, D], F32R)
        g_hi = sb("g_hi", [P, AHEAD, T], F32R)
        g_lo = sb("g_lo", [P, AHEAD, T], F32R)
        hot_i = sb("hot_i", [P, 2 * TOK, HALF])
        hot_j = sb("hot_j", [P, 2 * TOK, KEYS])
        picks = sb("picks", [P, 3, T])
        cf = sb("cf", [P, CF_COLS])
        cb = sb("cb", [P, CB_COLS], BF16)
        gain = sb("gain", [P, 2 * DEPTH, C])
        sink = sb("sink", [P, SWA_HEADS])
        neg_sink = sb("neg_sink", [P, SWA_HEADS])
        lamc = sb("lamc", [P, 2])
        bias_f = sb("bias_f", [P, 1])
        ms = sb("ms", [P, 8])
        root = sb("root", [P, 8])
        rstd = sb("rstd", [P, 8])
        newton = sb("newton", [P, 8])
        neg_max = sb("neg_max", [P, 2, 4])
        den = sb("den", [P, 4, 4])
        rden = sb("rden", [P, 4, 4])
        sink_e = sb("sink_e", [P, 4, 4])
        lsum = sb("lsum", [P, 2])

        def scratch(at, *shape, dt=F32):
            size = int(np.prod(shape))
            v = act[:, at:at + size]
            if dt != F32:
                v = v.bitcast(dt)
            names = "abcd"[:len(shape)]
            if len(shape) > 1:
                v = v.rearrange(f"p ({' '.join(names)}) -> p {' '.join(names)}",
                                **{n: s for n, s in zip(names[1:], shape[1:])})
            return v

        hf = scratch(0, C, T)
        y = scratch(2048, TT, D)
        pq_t = scratch(4096, HC, T)
        keys = scratch(8192, HC, KEYS)
        mix = scratch(10240, TT, D)
        g_fin = scratch(12288, D)
        lam_s = scratch(13312, 4, HD)
        lam_p = scratch(13568, 2, HD)
        sub_g = scratch(13696, P)
        cum = scratch(13824, T)
        ones = scratch(14080, T)
        moving_f = scratch(14336, T)
        fz = scratch(14592, T)
        fa = scratch(14848, T)
        fe = scratch(15104, T)
        fl = scratch(15360, T)
        wf_s = scratch(8192 - D, C, P)
        station_f = scratch(4096, FOX_HEADS, T)
        vd_n = scratch(6144, TT, 512)
        H2 = HALF * T
        k_pad = scratch(H2, 2, 8, T)
        v_n = scratch(H2 + 4096, TT, 512)
        qk_n = scratch(H2 + 5120, TT, 20 * HD)
        q_t = scratch(H2 + 7680, 8, T)
        fox_q = scratch(H2 + 9728, 4, T)
        ex = scratch(H2 + 10752, 2, 512)
        pr = scratch(H2 + 11776, 2, 256)
        p_t = scratch(H2 + 12288, 2, 512)
        rope_c = scratch(H2 + 13312, 20, 2, ROT // 2)
        rope_s = scratch(H2 + 13632, 20, 2, ROT // 2)
        dsq = scratch(H2 + 13952, TT, DIFF_HEADS, P)
        cb_in = scratch(H2 + 14976, CB_COLS)
        sc = scratch(H2, TT, HC, KEYS)
        sc2 = scratch(H2 + 4096, 2, KEYS)
        cand = scratch(H2 + 4352, 2, TOPK, TOPK)
        cand2 = scratch(H2 + 4864, 2, TOPK * TOPK)
        sv = scratch(H2 + 5376, TT, HC, TOPK)
        si = scratch(H2 + 5888, TT, HC, TOPK, dt=U32)
        sif = scratch(H2 + 6400, TT, HC, TOPK)
        tv = scratch(H2 + 6912, TT, P)
        tp = scratch(H2 + 7168, TT, P, dt=U32)
        ab_u = scratch(H2 + 7424, 2, TT * P, dt=U32)
        ab_f = scratch(H2 + 7936, 2, TT, P)
        tsum = scratch(H2 + 8448, TT * PEER_HEADS)
        pk = scratch(H2 + 8512, 3, TT, P)
        eq = scratch(H2 + 9280, P, TOPK)

        ps_a = psum("ps_a", [P, 2, 512])
        ps_o = psum("ps_o", [P, 4, 512])
        ps_s = psum("ps_s", [P, 2, 512])

        ident = cf[:, CF["ident"]]
        iota = cf[:, CF["iota"]]
        ident_b = cb[:, CB["ident"]]

        raw_full = [sem(f"raw_full{s}") for s in range(RAW)]
        hi_done = sem("hi_done")
        lo_done = sem("lo_done")
        chunk_used = sem("chunk_used")
        pair_out = sem("pair_out")
        loads = sem("loads")
        keys_in = sem("keys_in")
        masks_ready = sem("masks_ready")
        late_in = sem("late_in")
        zeroed = sem("zeroed")
        x_in = sem("x_in")
        x_new = sem("x_new")
        sq_done = sem("sq_done")
        ms_ready = sem("ms_ready")
        root_done = sem("root_done")
        y_ready = sem("y_ready")
        turned = sem("turned")
        hf_ready = sem("hf_ready")
        h_hi_done = sem("h_hi_done")
        h_ready = sem("h_ready")
        f_done = sem("f_done")
        f_abs = sem("f_abs")
        f_exp = sem("f_exp")
        f_ln = sem("f_ln")
        f_ready = sem("f_ready")
        lam_ready = sem("lam_ready")
        lam_exp = sem("lam_exp")
        roped = sem("roped")
        qk_turned = sem("qk_turned")
        qk_ready = sem("qk_ready")
        logits_done = sem("logits_done")
        max_done = sem("max_done")
        exp_done = sem("exp_done")
        probs_ready = sem("probs_ready")
        p_turned = sem("p_turned")
        p_t_ready = sem("p_t_ready")
        pv_done = sem("pv_done")
        pv_out = sem("pv_out")
        scores_done = sem("scores_done")
        scores_out = sem("scores_out")
        top_sub = sem("top_sub")
        top_exp = sem("top_exp")
        picks_ready = sem("picks_ready")
        picks_turned = sem("picks_turned")
        picks_out = sem("picks_out")
        hots_ready = sem("hots_ready")
        hots_used = sem("hots_used")
        gated = sem("gated")
        g_hi_done = sem("g_hi_done")
        g_lo_done = sem("g_lo_done")
        y_out = sem("y_out")
        stored = sem("stored")
        dve_step = sem("dve_step")
        act_step = sem("act_step")

        N_LOADS = 6
        norm_of = {("in", l): 2 * l for l in range(DEPTH)} | {("pq", l): 2 * l + 1 for l in range(DEPTH)}
        turn_of = {(s, l): 3 * l + k for l in range(DEPTH) for k, s in enumerate(("in", "out", "pq"))}

        def pair_index(l, seg, k=0):
            return (START[seg, l] - l * KEYS + k) // 2

        def ps_block(k):
            return ps_a[:, k % 4 // 2, (k % 2) * T:(k % 2 + 1) * T]

        block = ctx.enter_context(nc.Block())

        @block.sync
        def _(sp):
            for tt in range(TT):
                sp.dma_start(xs[:, tt, :], x[tt * P:(tt + 1) * P, :]).then_inc(x_in, 16)

            def load(n, src):
                if not isinstance(n, int) or n >= RAW:
                    sp.wait_ge(lo_done, n - RAW + 1)
                sp.dma_start(raw[:, slot, :], src).then_inc(raw_full[slot], 16)

            for l in range(DEPTH):
                for seg, w in (("in", w_c if l else w_ab), ("out", w_c_out if l else w_ab_out), ("pq", w_pq[l])):
                    for k in range(w.shape[0]):
                        slot = k % RAW
                        load(START[seg, l] + k, w[k])
                for seg, w in (("u", u_t[l]), ("v", v_e[l])):
                    with sp.Fori(0, KEYS // RAW) as turn:
                        for slot in range(RAW):
                            load(turn * RAW + START[seg, l] + slot, w[bass.ds(turn * RAW + slot, 1)].rearrange("a p n -> (a p) n"))
            for tt in range(TT):
                sp.wait_ge(y_out, tt + 1)
                sp.dma_start(out[tt * P:(tt + 1) * P, :], y[:, tt, :]).then_inc(stored, 16)
            sp.wait_ge(stored, 16 * TT)

        @block.gpsimd
        def _(pool):
            pool.memset(wf_s, 0.0).then_inc(zeroed, 1)
            pool.memset(bias_f[:], 0.0).then_inc(zeroed, 1)
            pool.memset(ones, 1.0).then_inc(zeroed, 1)
            pool.dma_start(cf[:], consts).then_inc(loads, 16)
            pool.dma_start(cb_in, masks).then_inc(loads, 16)
            pool.dma_start(gain[:], gains).then_inc(loads, 16)
            pool.dma_start(sink[:], sinks.partition_broadcast(P)).then_inc(loads, 16)
            pool.dma_start(lam_s, lam_vecs.partition_broadcast(P)).then_inc(loads, 16)
            pool.dma_start(sub_g, subln.partition_broadcast(P)).then_inc(loads, 16)
            pool.dma_start(keys, keys_t[0]).then_inc(keys_in, 16)
            pool.memset(k_pad, 0.0).then_inc(zeroed, 1)
            pool.wait_ge(zeroed, 4)
            for r in (0, 32):
                pool.dma_start(wf_s[:, :, r:r + FOX_HEADS], w_f).then_inc(late_in, 16)
                pool.dma_start(bias_f[r:r + FOX_HEADS, :], f_bias).then_inc(late_in, 16)
            pool.memset(newton[:], 0.0).then_inc(hots_used, 2)
            pool.memset(root[:], 0.0).then_inc(gated, 2)
            pool.wait_ge(x_new, 8)
            pool.dma_start(keys, keys_t[1]).then_inc(keys_in, 16)
            pool.memset(k_pad, 0.0).then_inc(zeroed, 1)
            pool.wait_ge(x_new, 16)
            pool.dma_start(g_fin, gain_final.partition_broadcast(P)).then_inc(late_in, 16)

        @block.scalar
        def _(sc_e):
            steps = [0]

            def link(ins):
                steps[0] += 1
                ins.then_inc(act_step, 1)
                sc_e.wait_ge(act_step, steps[0])

            def split_hi(n, slot, waits_used=True):
                if isinstance(n, int):
                    if n >= CHUNKS:
                        return
                    sc_e.wait_ge(raw_full[slot % RAW], 16 * (n // RAW + 1))
                if waits_used:
                    sc_e.wait_ge(chunk_used, n - AHEAD + 1)
                sc_e.activation(w_hi[:, slot % AHEAD, :], raw[:, slot % RAW, :], ACT.Copy).then_inc(hi_done, 1)

            def norm_squares(k):
                if k:
                    sc_e.wait_ge(x_new, 4 * k)
                else:
                    sc_e.wait_ge(x_in, 16 * TT)
                for tt in range(TT):
                    sc_e.activation(y[:, tt, :], xs[:, tt, :], ACT.Square, accum_out=rstd[:, tt:tt + 1]).then_inc(sq_done, 1)
                sc_e.wait_ge(ms_ready, MS_VALUE[k])
                sc_e.activation(root[:, 0:TT], ms[:, 0:TT], ACT.Sqrt).then_inc(root_done, 1)

            MS_VALUE = [1, 3, 4, 5, 6]

            def operand_hi(s):
                for half in range(2):
                    sc_e.wait_ge(hf_ready, 4 * s + 2 * half + 2)
                    c = slice(4 * half, 4 * half + 4)
                    sc_e.activation(h_hi[:, c, :], hf[:, c, :], ACT.Copy).then_inc(h_hi_done, 1)

            def turned_out(l, count):
                for b in range(count):
                    sc_e.wait_ge(qk_turned, 4 * l + b + 1)
                    two = ps_o[:, b % 4, :].rearrange("p (b t) -> p b t", b=2)
                    if b < count - (1 if l else 2):
                        sc_e.activation(q_t[:, 2 * b:2 * b + 2, :], two, ACT.Copy).then_inc(qk_ready, 1)
                    else:
                        keys_out(0 if l else 2 * b, two).then_inc(qk_ready, 1)

            def keys_out(at, two):
                sc_e.activation(k_pad[0:HD, 0, at:at + 2, :], two[0:HD], ACT.Copy)
                return sc_e.activation(k_pad[HD:P, 1, at:at + 2, :], two[HD:P], ACT.Copy)

            def pair(b):
                return ps_a[:, b % 2, :]

            def attention(l):
                base = len(UNITS[0]) * l
                for k, (kind, tile, heads) in enumerate(UNITS[l]):
                    u = base + k
                    maps = 4 if tile == 0 else 2
                    nk = 512 // maps
                    sc_e.wait_ge(max_done, u + 1)
                    if u >= 2:
                        sc_e.wait_ge(p_turned, u - 1)
                    if kind == "swa":
                        sc_e.activation(sink_e[:, u % 4, 0:maps], sink_e[:, u % 4, 0:maps], ACT.Exp).then_inc(exp_done, 1)
                    for m in range(maps):
                        ins = sc_e.activation(ex[:, u % 2, m * nk:(m + 1) * nk], ps_o[:, u % 2, m * nk:(m + 1) * nk],
                                              ACT.Exp, bias=neg_max[:, u % 2, m:m + 1], scale=HD ** -0.5,
                                              accum_out=den[:, u % 4, m:m + 1])
                    ins.then_inc(exp_done, 1)

            for n in range(AHEAD):
                split_hi(n, n, waits_used=False)
            for l in range(DEPTH):
                norm_squares(norm_of["in", l])
                operand_hi(turn_of["in", l])
                if l == 0:
                    sc_e.wait_ge(f_abs, 1)
                    sc_e.activation(fe, fa, ACT.Exp, scale=-1.0).then_inc(f_exp, 1)
                    sc_e.wait_ge(f_exp, 1)
                    sc_e.activation(fl, fe, ACT.Ln, bias=1.0).then_inc(f_ln, 1)
                    sc_e.wait_ge(lam_ready, 1)
                    sc_e.activation(lsum[:], lsum[:], ACT.Exp).then_inc(lam_exp, 1)
                sc_e.wait_ge(zeroed, 4 + l)
                blocks = C_BLOCKS if l else AB_BLOCKS
                for k in range(blocks):
                    n = START["in", l] + k
                    split_hi(n + AHEAD, k + AHEAD)
                    if k % 2:
                        sc_e.wait_ge(chunk_used, n + 1)
                        b = k // 2
                        two = pair(pair_index(l, "in", k - 1))
                        rows = two.rearrange("p (b t c) -> p t b c", b=2, t=TT)
                        if l == 0:
                            lanes = [(fox_q, None)] * 4 + [(v_n, 4)] * 2 + [(qk_n, 6)] * 4 + [(vd_n, 10)] * 2
                        else:
                            lanes = [(qk_n, 0)] * 5 + [(v_n, 5)]
                        to, first = lanes[b]
                        if first is None and b < 2:
                            sc_e.activation(to[:, 2 * b:2 * b + 2, :], two.rearrange("p (b t) -> p b t", b=2), ACT.Copy)\
                                .then_inc(pair_out, 1)
                        elif first is None:
                            keys_out(2 * b - 4, two.rearrange("p (b t) -> p b t", b=2)).then_inc(pair_out, 1)
                        else:
                            dst = to[:, :, (b - first) * T:(b - first + 1) * T].rearrange("p t (b c) -> p t b c", b=2)
                            sc_e.activation(dst, rows, ACT.Copy).then_inc(pair_out, 1)
                turned_out(l, 5 if l else 4)
                attention(l)
                if l == 0:
                    sc_e.wait_ge(ms_ready, 2)
                    sc_e.activation(root[:], ms[:], ACT.Sqrt).then_inc(root_done, 1)
                operand_hi(turn_of["out", l])
                for k in range(OUT_BLOCKS):
                    split_hi(START["out", l] + k + AHEAD, k + AHEAD)
                norm_squares(norm_of["pq", l])
                operand_hi(turn_of["pq", l])
                for k in range(PQ_BLOCKS):
                    n = START["pq", l] + k
                    split_hi(n + AHEAD, k + AHEAD)
                    if k % 2:
                        sc_e.wait_ge(chunk_used, n + 1)
                        sc_e.activation(pq_t[:, k - 1:k + 1, :],
                                        pair(pair_index(l, "pq", k - 1)).rearrange("p (b t) -> p b t", b=2), ACT.Copy)\
                            .then_inc(pair_out, 1)
                for b in range(2 * 4):
                    sc_e.wait_ge(scores_done, 8 * l + b + 1)
                    sc_e.activation(sc[:, b // 4, 4 * (b % 4):4 * (b % 4) + 4, :],
                                    ps_o[:, b % 4, :].rearrange("p (k e) -> p k e", k=4), ACT.Copy).then_inc(scores_out, 1)

                def u_chunks(turn, i0):
                    for s in range(RAW):
                        n = turn * RAW + (START["u", l] + i0 + s)
                        sc_e.wait_ge(raw_full[(s + AHEAD) % RAW],
                                     turn * 16 + 16 * ((START["u", l] + i0 + s + AHEAD) // RAW + 1))
                        sc_e.wait_ge(chunk_used, n + 1)
                        sc_e.activation(w_hi[:, s % AHEAD, :], raw[:, (s + AHEAD) % RAW, :], ACT.Copy).then_inc(hi_done, 1)
                        if s % 2:
                            at = turn * (RAW * T) + (i0 + s - 1) * T
                            sc_e.activation(act[:, bass.ds(at, 2 * T)], ps_a[:, s // 2, :], ACT.Gelu_apprx_tanh)\
                                .then_inc(pair_out, 1)

                with sc_e.Fori(0, TURNS - 2) as turn:
                    u_chunks(turn, 0)
                sc_e.wait_ge(top_sub, l + 1)
                sc_e.activation(pk[:, 2], pk[:, 2], ACT.Exp).then_inc(top_exp, 1)
                with sc_e.Fori(0, 2) as turn:
                    u_chunks(turn, HALF - 2 * RAW)
                with sc_e.Fori(0, TURNS) as turn:
                    u_chunks(turn, HALF)

                def g_rounded(i, slot):
                    sc_e.activation(g_hi[:, slot, :], act[:, bass.ds(i * T, T)], ACT.Copy).then_inc(g_hi_done, 1)

                for half in range(2):
                    i0 = half * HALF
                    sc_e.wait_ge(gated, 2 + (2 * l + half + 1) * (T // 8))
                    sc_e.wait_ge(chunk_used, START["v", l] + i0)
                    for s in range(AHEAD):
                        g_rounded(i0 + s, s)
                    with sc_e.Fori(0, TURNS - 1) as turn:
                        for s in range(RAW):
                            n0 = START["v", l] + i0 + s
                            sc_e.wait_ge(raw_full[(s + AHEAD) % RAW], turn * 16 + 16 * ((n0 + AHEAD) // RAW + 1))
                            sc_e.wait_ge(chunk_used, turn * RAW + n0 + 1)
                            sc_e.activation(w_hi[:, s % AHEAD, :], raw[:, (s + AHEAD) % RAW, :], ACT.Copy)\
                                .then_inc(hi_done, 1)
                            g_rounded(turn * RAW + (i0 + s + AHEAD), s % AHEAD)
                    for s in range(RAW):
                        i = i0 + HALF - RAW + s
                        split_hi(START["v", l] + i + AHEAD, i + AHEAD)
                        if s + AHEAD < RAW:
                            sc_e.wait_ge(chunk_used, START["v", l] + i + 1)
                            g_rounded(i + AHEAD, s % AHEAD)
            norm_squares(4)

        @block.vector
        def _(dve):
            steps = [0]

            def link(ins):
                steps[0] += 1
                ins.then_inc(dve_step, 1)
                dve.wait_ge(dve_step, steps[0])

            def rest_lo(n, slot):
                if isinstance(n, int) and n >= CHUNKS:
                    return
                dve.wait_ge(hi_done, n + 1)
                dve.tensor_tensor(w_lo[:, slot % AHEAD, :], raw[:, slot % RAW, :], w_hi[:, slot % AHEAD, :].bitcast(F32),
                                  ALU.subtract).then_inc(lo_done, 1)

            def inverse_root(n, count):
                dve.wait_ge(root_done, n)
                r, m, t = rstd[:, 0:count], ms[:, 0:count], newton[:, 0:count]
                link(dve.reciprocal(r, root[:, 0:count]))
                link(dve.tensor_tensor(t, r, r, ALU.mult))
                link(dve.tensor_tensor(t, t, m, ALU.mult))
                link(dve.tensor_scalar(t, t, -0.5, 1.5, ALU.mult, ALU.add))
                link(dve.tensor_tensor(r, r, t, ALU.mult))

            def norm_rows(k, n):
                dve.wait_ge(sq_done, TT * (k + 1))
                dve.tensor_scalar(ms[:, 0:TT], rstd[:, 0:TT], 1.0 / D, EPS, ALU.mult, ALU.add).then_inc(ms_ready, 1)
                inverse_root(n, TT)

            def operand(s, g=None):
                for b in range(4):
                    dve.wait_ge(turned, 4 * s + b + 1)
                    src = ps_o[:, b, :].rearrange("p (c t) -> p c t", c=2)
                    dst = hf[:, 2 * b:2 * b + 2, :]
                    if g is None:
                        dve.tensor_copy(dst, src).then_inc(hf_ready, 1)
                    else:
                        dve.tensor_tensor(dst, src, g[:, 2 * b:2 * b + 2].unsqueeze(2).to_broadcast([P, 2, T]),
                                          ALU.mult).then_inc(hf_ready, 1)
                for half in range(2):
                    dve.wait_ge(h_hi_done, 2 * s + half + 1)
                    c = slice(4 * half, 4 * half + 4)
                    dve.tensor_tensor(h_lo[:, c, :], hf[:, c, :], h_hi[:, c, :].bitcast(F32), ALU.subtract)\
                        .then_inc(h_ready, 1)

            def norm(k, n, s):
                norm_rows(k, n)
                for tt in range(TT):
                    dve.tensor_scalar(y[:, tt, :], xs[:, tt, :], rstd[:, tt:tt + 1], None, ALU.mult).then_inc(y_ready, 1)
                operand(s, gain[:, k, :])

            def fox_gates():
                dve.wait_ge(f_done, 1)
                dve.wait_ge(late_in, 64)
                link(dve.tensor_scalar(fz, ps_s[:, 0, 0:T], bias_f[:, 0:1], None, ALU.add))
                dve.scalar_tensor_tensor(out=fa, in0=fz, scalar=-1.0, in1=fz, op0=ALU.mult, op1=ALU.max).then_inc(f_abs, 1)
                dve.wait_ge(f_ln, 1)
                link(dve.scalar_tensor_tensor(out=fz, in0=fz, scalar=0.0, in1=fl, op0=ALU.min, op1=ALU.subtract))
                link(dve.tensor_tensor_scan(cum, ones, fz, 0.0, ALU.mult, ALU.add))
                dve.tensor_scalar(moving_f, cum, cf[:, CF["mv_scale"]], cf[:, CF["mv_add"]], ALU.mult, ALU.add)
                shape = [P, FOX_HEADS, T]
                link(dve.tensor_tensor(station_f, cum.unsqueeze(1).to_broadcast(shape),
                                       cf[:, CF["st_scale"]].unsqueeze(2).to_broadcast(shape), ALU.mult))
                dve.tensor_tensor(station_f, station_f, cf[:, CF["st_add"]].unsqueeze(2).to_broadcast(shape),
                                  ALU.add).then_inc(f_ready, 1)

            def lambda_row():
                dve.tensor_tensor(lam_p[:, 0, :], lam_s[:, 0, :], lam_s[:, 1, :], ALU.mult)
                link(dve.tensor_tensor(lam_p[:, 1, :], lam_s[:, 2, :], lam_s[:, 3, :], ALU.mult))
                dve.tensor_reduce(lsum[:], lam_p, AX_X, ALU.add).then_inc(lam_ready, 1)
                dve.wait_ge(lam_exp, 1)
                dve.memset(lamc[:, 0:1], 1.0)
                link(dve.tensor_tensor(lamc[:, 1:2], lsum[:, 1:2], lsum[:, 0:1], ALU.subtract))
                link(dve.tensor_scalar(lamc[:, 1:2], lamc[:, 1:2], -LAM_INIT, None, ALU.add))

            def rope(heads):
                for tt in range(TT):
                    both = qk_n[:, tt, 0:heads * HD].rearrange("p (h e) -> p h e", e=HD)[:, :, 0:ROT]
                    both = both.rearrange("p h (a r) -> p h a r", a=2)
                    shape = [P, heads, 2, ROT // 2]
                    for table, to in (("cos", rope_c), ("sin", rope_s)):
                        t = cf[:, CF[table]].rearrange("p (t r) -> p t r", t=TT)[:, tt, :]
                        ins = dve.tensor_tensor(to[:, 0:heads], both, t.unsqueeze(1).unsqueeze(1).to_broadcast(shape), ALU.mult)
                    link(ins)
                    dve.tensor_tensor(both[:, :, 0, :], rope_c[:, 0:heads, 0, :], rope_s[:, 0:heads, 1, :], ALU.subtract)
                    link(dve.tensor_tensor(both[:, :, 1, :], rope_c[:, 0:heads, 1, :], rope_s[:, 0:heads, 0, :], ALU.add))
                dve.sem_inc(roped, 1)

            def attention(l):
                base = len(UNITS[0]) * l
                units = UNITS[l]

                def exps(u):
                    return u + 1 if l == 0 else base + 2 * (u - base + 1)

                def maxima(k):
                    kind, tile, heads = units[k]
                    u, maps = base + k, 4 if tile == 0 else 2
                    dve.wait_ge(logits_done, u + 1)
                    m = neg_max[:, u % 2, 0:maps]
                    link(dve.tensor_reduce(m, ps_o[:, u % 2, :].rearrange("p (m k) -> p m k", m=maps), AX_X, ALU.max))
                    ins = dve.tensor_scalar(m, m, -HD ** -0.5, None, ALU.mult)
                    if kind == "swa":
                        h = slice(heads[0], heads[0] + maps)
                        link(ins)
                        link(dve.tensor_tensor(m, m, neg_sink[:, h], ALU.min))
                        ins = dve.tensor_tensor(sink_e[:, u % 4, 0:maps], sink[:, h], m, ALU.add)
                    ins.then_inc(max_done, 1)

                def inverses(k):
                    kind, tile, heads = units[k]
                    u, maps = base + k, 4 if tile == 0 else 2
                    dve.wait_ge(exp_done, exps(u))
                    d, r = den[:, u % 4, 0:maps], rden[:, u % 4, 0:maps]
                    if kind == "swa":
                        link(dve.tensor_tensor(d, d, sink_e[:, u % 4, 0:maps], ALU.add))
                    link(dve.reciprocal(r, d))
                    if kind == "diff":
                        n = maps // 2
                        r2 = r.rearrange("p (h j) -> p h j", j=2)
                        link(dve.tensor_tensor(r2, r2, lamc[:].unsqueeze(1).to_broadcast([P, n, 2]), ALU.mult))
                        e = ex[:, u % 2, :].rearrange("p (m k) -> p m k", m=maps)
                        link(dve.tensor_tensor(e, e, r.unsqueeze(2).to_broadcast([P, maps, 512 // maps]), ALU.mult))
                        e = ex[:, u % 2, :].rearrange("p (h j k) -> p h j k", j=2, h=n)
                        if u >= 2:
                            dve.wait_ge(p_turned, u - 1)
                        dve.tensor_tensor(pr[:, u % 2, :].rearrange("p (h k) -> p h k", h=n), e[:, :, 0], e[:, :, 1],
                                          ALU.add).then_inc(probs_ready, 1)

                def p_t_out(k):
                    kind, tile, heads = units[k]
                    u = base + k
                    w = 256 if kind == "diff" else 512
                    dve.wait_ge(p_turned, u + 1)
                    if u >= 2:
                        dve.wait_ge(pv_done, u - 1)
                    dve.tensor_copy(p_t[:, u % 2, 0:w], ps_o[:, 2 + u % 2, 0:w]).then_inc(p_t_ready, 1)

                def values_out(k):
                    kind, tile, heads = units[k]
                    u, n = base + k, len(heads)
                    dve.wait_ge(pv_done, u + 1)
                    if kind == "diff":
                        dst = mix[:, tile, 512 + heads[0] * P:512 + (heads[0] + n) * P]
                        dve.tensor_copy(dst, ps_s[:, u % 2, 0:n * P]).then_inc(pv_out, 1)
                    else:
                        dst = mix[:, tile, heads[0] * HD:(heads[0] + n) * HD].rearrange("p (m e) -> p m e", m=n)
                        dve.tensor_tensor(dst, ps_s[:, u % 2, 0:n * HD].rearrange("p (m e) -> p m e", m=n),
                                          rden[:, u % 4, 0:n].unsqueeze(2).to_broadcast([P, n, HD]), ALU.mult)\
                            .then_inc(pv_out, 1)

                for k in range(len(units) + 2):
                    if k < len(units):
                        maxima(k)
                    if 0 <= k - 1 < len(units):
                        inverses(k - 1)
                        p_t_out(k - 1)
                    if k >= 2:
                        values_out(k - 2)

            def diff_norm():
                dve.wait_ge(pv_out, len(UNITS[0]))
                o = mix[:, :, 512:1024].rearrange("p t (h e) -> p t h e", h=DIFF_HEADS)
                link(dve.tensor_tensor(dsq, o, o, ALU.mult))
                link(dve.tensor_reduce(ms[:].rearrange("p (t h) -> p t h", t=TT), dsq, AX_X, ALU.add))
                dve.tensor_scalar(ms[:], ms[:], 1.0 / P, EPS, ALU.mult, ALU.add).then_inc(ms_ready, 1)
                link(dve.tensor_scalar(sub_g, sub_g, 1.0 - LAM_INIT, None, ALU.mult))
                inverse_root(2, 8)
                r = rstd[:].rearrange("p (t h) -> p t h", t=TT)
                shape = [P, TT, DIFF_HEADS, P]
                link(dve.tensor_tensor(o, o, r.unsqueeze(3).to_broadcast(shape), ALU.mult))
                link(dve.tensor_tensor(o, o, sub_g.unsqueeze(1).unsqueeze(1).to_broadcast(shape), ALU.mult))

            def top16(values, indices, src, spare):
                link(dve.max(values[:, 0:8], src))
                dve.max_index(indices[:, 0:8], values[:, 0:8], src)
                link(dve.match_replace(spare, values[:, 0:8], src, REPLACED))
                link(dve.max(values[:, 8:16], spare))
                link(dve.max_index(indices[:, 8:16], values[:, 8:16], spare))

            def select(l, i):
                lists = TT * HC
                finals = TT * PEER_HEADS
                if i < lists:
                    tt, k = divmod(i, HC)
                    dve.wait_ge(scores_out, 8 * l + 4 * tt + k // 4 + 1)
                    top16(sv[:, tt, k, :], si[:, tt, k, :], sc[:, tt, k, :], sc2[:, i % 2, :])
                elif i < lists + finals:
                    tt, h = divmod(i - lists, PEER_HEADS)
                    shape = [P, TOPK, TOPK]
                    link(dve.tensor_tensor(cand[:, i % 2], sv[:, tt, 2 * h, :].unsqueeze(2).to_broadcast(shape),
                                           sv[:, tt, 2 * h + 1, :].unsqueeze(1).to_broadcast(shape), ALU.add))
                    top16(tv[:, tt, h * TOPK:(h + 1) * TOPK], tp[:, tt, h * TOPK:(h + 1) * TOPK],
                          cand[:, i % 2].rearrange("p a b -> p (a b)"), cand2[:, i % 2, :])
                elif i == lists + finals:
                    t = tv.rearrange("p t (h k) -> p (t h) k", k=TOPK)
                    w = pk[:, 2].rearrange("p t (h k) -> p (t h) k", k=TOPK)
                    dve.tensor_tensor(w, t, t[:, :, 0:1].to_broadcast([P, finals, TOPK]), ALU.subtract).then_inc(top_sub, 1)
                    flat = tp.rearrange("p t k -> p (t k)")
                    dve.tensor_scalar(ab_u[:, 0], flat, 4, None, ALU.logical_shift_right)
                    link(dve.tensor_scalar(ab_u[:, 1], flat, TOPK - 1, None, ALU.bitwise_and))
                    dve.tensor_copy(ab_f.rearrange("p s t k -> p s (t k)"), ab_u)
                    link(dve.tensor_copy(sif, si))
                elif i < lists + finals + 13:
                    which, step = divmod(i - lists - finals - 1, 3)
                    tt, side = divmod(which, 2)
                    if step == 0:
                        link(dve.tensor_tensor(eq, ab_f[:, side, tt, :].unsqueeze(2).to_broadcast([P, P, TOPK]),
                                               iota[:, 0:TOPK].unsqueeze(1).to_broadcast([P, P, TOPK]), ALU.is_equal))
                    elif step == 1:
                        e4 = eq.rearrange("p (h k) a -> p h k a", h=PEER_HEADS)
                        held = sif[:, tt].rearrange("p (h s) a -> p h s a", s=2)[:, :, side, :]
                        link(dve.tensor_tensor(e4, e4, held.unsqueeze(2).to_broadcast([P, PEER_HEADS, TOPK, TOPK]), ALU.mult))
                    else:
                        link(dve.tensor_reduce(pk[:, side, tt, :], eq, AX_X, ALU.add))
                elif i == lists + finals + 13:
                    dve.wait_ge(top_exp, l + 1)
                    w = pk[:, 2].rearrange("p t (h k) -> p (t h) k", k=TOPK)
                    link(dve.tensor_reduce(tsum, w, AX_X, ALU.add))
                    link(dve.reciprocal(tsum, tsum))
                    dve.tensor_tensor(w, w, tsum.unsqueeze(2).to_broadcast([P, finals, TOPK]), ALU.mult).then_inc(picks_ready, 1)

            def one_hots(half, group, static):
                for k in range(TOK):
                    s = static * TOK + k
                    t = group * TOK + k
                    dve.tensor_scalar(hot_j[:, s, :], iota, picks[:, 1, bass.ds(t, 1)], None, ALU.is_equal)
                    ins = dve.tensor_scalar(hot_i[:, s, :], iota[:, half * HALF:(half + 1) * HALF],
                                            picks[:, 0, bass.ds(t, 1)], picks[:, 2, bass.ds(t, 1)], ALU.is_equal, ALU.mult)
                ins.then_inc(hots_ready, 1)

            def gate(half, bank, static):
                a = act[:, half * HALF * T:(half + 1) * HALF * T].rearrange("p (i t) -> p i t", t=T)[:, :, bass.ds(bank * 8, 8)]
                dve.tensor_tensor(a, a, ps_s[:, static, :].rearrange("p (t i) -> p i t", i=HALF), ALU.mult).then_inc(gated, 1)

            def scatter_turn(l, half, turn, n0, with_g, last):
                g0 = (2 * l + half) * HALF
                for s in range(RAW):
                    rest_lo(turn * RAW + n0 + s + AHEAD, s + AHEAD)
                    if with_g and not (last and s + AHEAD >= RAW):
                        g_rest(l, turn * RAW + s + AHEAD, s % AHEAD)
                    if not (last and s == RAW - 1):
                        dve.wait_ge(hots_used, turn * RAW + g0 + s + 2)
                        one_hots(half, turn * RAW + s + 1, (s + 1) % 2)
                    if s % 2:
                        dve.wait_ge(hots_used, turn * RAW + g0 + s + 3)
                        gate(half, turn * 2 + s // 2, s // 2 % 2)

            def g_rest(l, i, slot):
                dve.wait_ge(g_hi_done, i + KEYS * l + 1)
                dve.tensor_tensor(g_lo[:, slot, :], act[:, bass.ds(i * T, T)], g_hi[:, slot, :].bitcast(F32), ALU.subtract)\
                    .then_inc(g_lo_done, 1)

            dve.wait_ge(loads, 16 * N_LOADS)
            dve.tensor_copy(cb[:], cb_in).then_inc(masks_ready, 1)
            dve.wait_ge(x_in, 16 * TT)
            dve.wait_ge(zeroed, 3)
            dve.wait_ge(hots_used, 2)
            dve.wait_ge(gated, 2)
            for n in range(AHEAD):
                rest_lo(n, n)
            roots = [0]

            def next_root():
                roots[0] += 1
                return roots[0]

            for l in range(DEPTH):
                norm(2 * l, next_root(), turn_of["in", l])
                if l == 0:
                    fox_gates()
                    lambda_row()
                    next_root()
                for k in range(C_BLOCKS if l else AB_BLOCKS):
                    rest_lo(START["in", l] + k + AHEAD, k + AHEAD)
                dve.wait_ge(pair_out, pair_index(l, "in") + (10 if l == 0 else 5))
                rope(20 if l else 16)
                if l == 1:
                    link(dve.tensor_scalar(neg_sink[:], sink[:], -1.0, None, ALU.mult))
                attention(l)
                if l == 0:
                    diff_norm()
                dve.wait_ge(pv_out, len(UNITS[0]) * (l + 1))
                dve.sem_inc(y_ready, TT)
                operand(turn_of["out", l])
                for k in range(OUT_BLOCKS):
                    n = START["out", l] + k
                    rest_lo(n + AHEAD, k + AHEAD)
                    if k % 2:
                        dve.wait_ge(chunk_used, n + 1)
                        to = xs[:, :, (k - 1) * P:(k + 1) * P].rearrange("p t (b c) -> p t b c", b=2)
                        two = ps_a[:, pair_index(l, "out", k - 1) % 2, :].rearrange("p (b t c) -> p t b c", b=2, t=TT)
                        dve.tensor_tensor(to, to, two, ALU.add).then_inc(pair_out, 1)
                dve.wait_ge(pair_out, pair_index(l, "pq"))
                dve.sem_inc(x_new, 4)
                norm(2 * l + 1, next_root(), turn_of["pq", l])
                for k in range(PQ_BLOCKS):
                    rest_lo(START["pq", l] + k + AHEAD, k + AHEAD)
                for i in range(HALF):
                    select(l, i)
                    rest_lo(START["u", l] + i + AHEAD, i + AHEAD)
                dve.wait_ge(picks_turned, l + 1)
                dve.tensor_copy(picks[:, 0:2, :], ps_s[:, 0, :].rearrange("p (s t) -> p s t", s=2))
                dve.tensor_copy(picks[:, 2, :], ps_s[:, 1, 0:T]).then_inc(picks_out, 1)
                dve.wait_ge(picks_out, l + 1)
                for half in range(2):
                    n0 = START["u", l] + HALF if half == 0 else START["v", l]
                    dve.wait_ge(hots_used, (2 * l + half) * HALF + 1)
                    one_hots(half, 0, 0)
                    if half == 1:
                        for s in range(AHEAD):
                            g_rest(l, s, s)
                    with dve.Fori(0, TURNS - 1) as turn:
                        scatter_turn(l, half, turn, n0, half == 1, False)
                    scatter_turn(l, half, TURNS - 1, n0, half == 1, True)
                for s in range(AHEAD):
                    g_rest(l, HALF + s, s)
                n0 = START["v", l] + HALF
                with dve.Fori(0, TURNS - 1) as turn:
                    for s in range(RAW):
                        rest_lo(turn * RAW + n0 + s + AHEAD, s + AHEAD)
                        g_rest(l, turn * RAW + HALF + s + AHEAD, s % AHEAD)
                for s in range(RAW):
                    rest_lo(n0 + HALF - RAW + s + AHEAD, s + AHEAD)
                    if s + AHEAD < RAW:
                        g_rest(l, KEYS - RAW + s + AHEAD, s)
                dve.wait_ge(chunk_used, START["v", l] + KEYS)
                for b in range(4):
                    to = xs[:, b // 2, (b % 2) * 512:(b % 2 + 1) * 512]
                    dve.tensor_tensor(to, to, ps_o[:, b, :], ALU.add).then_inc(x_new, 1)
                dve.wait_ge(x_new, 8 * l + 8)
            norm_rows(4, next_root())
            dve.wait_ge(late_in, 80)
            for tt in range(TT):
                dve.scalar_tensor_tensor(out=y[:, tt, :], in0=xs[:, tt, :], scalar=rstd[:, tt:tt + 1], in1=g_fin,
                                         op0=ALU.mult, op1=ALU.mult).then_inc(y_out, 1)

        @block.tensor
        def _(pe):
            def transposed_block(n, k):
                o = ps_block(k)
                for c in range(C):
                    cols = slice(c * P, (c + 1) * P)
                    hi, lo = w_hi[:, k % AHEAD, cols], w_lo[:, k % AHEAD, cols]
                    pe.matmul(o, hi, h_hi[:, c, :], start=(c == 0), stop=False)
                    pe.matmul(o, hi, h_lo[:, c, :], start=False, stop=False)
                    ins = pe.matmul(o, lo, h_hi[:, c, :], start=False, stop=(c == C - 1))
                ins.then_inc(chunk_used, 1)

            def row_block(n, k):
                for tt in range(TT):
                    o = ps_block(k)[:, tt * P:(tt + 1) * P]
                    t = slice(tt * P, (tt + 1) * P)
                    for c in range(C):
                        cols = slice(c * P, (c + 1) * P)
                        hi, lo = w_hi[:, k % AHEAD, cols], w_lo[:, k % AHEAD, cols]
                        pe.matmul(o, h_hi[:, c, t], hi, start=(c == 0), stop=False)
                        pe.matmul(o, h_hi[:, c, t], lo, start=False, stop=False)
                        ins = pe.matmul(o, h_lo[:, c, t], hi, start=False, stop=(c == C - 1))
                ins.then_inc(chunk_used, 1)

            def turn_rows(s, src, count):
                pe.wait_ge(y_ready, count)
                for c in range(C):
                    for tt in range(TT):
                        ins = pe.transpose(ps_o[:, c // 2, (c % 2) * T + tt * P:(c % 2) * T + (tt + 1) * P],
                                           src[:, tt, c * P:(c + 1) * P], ident)
                    if c % 2:
                        ins.then_inc(turned, 1)

            def segment(l, seg, count, kinds):
                for k in range(count):
                    n = START[seg, l] + k
                    pe.wait_ge(lo_done, n + 1)
                    p = pair_index(l, seg, k)
                    if k % 2 == 0 and p >= 2:
                        pe.wait_ge(pair_out, p - 1)
                    (transposed_block if kinds[k] == "T" else row_block)(n, k)

            def turn_queries(l):
                pe.wait_ge(roped, l + 1)
                for b in range(10 if l else 8):
                    if b == 8:
                        pe.wait_ge(qk_ready, 4 * l + 1)
                    for tt in range(TT):
                        src = qk_n[:, tt, b * P:(b + 1) * P]
                        at = (b % 2) * T + tt * P
                        ins = pe.transpose(ps_o[:, b // 2 % 4, at:at + P], src, ident)
                    if b % 2:
                        ins.then_inc(qk_turned, 1)

            def attention(l):
                base = len(UNITS[0]) * l
                units = UNITS[l]

                def operands(kind, h, j):
                    if kind == "fox":
                        return fox_q[:, h // 2, :], k_pad[:, h % 2, h // 2, :]
                    if kind == "diff":
                        return q_t[:, h, :], k_pad[:, j, DIFF_HEADS + h, :]
                    g = h // 4
                    return q_t[:, h % 4 + 4 * (g // 2), :], k_pad[:, g % 2, g // 2, :]

                def logits(k):
                    kind, tile, heads = units[k]
                    u, maps = base + k, 4 if tile == 0 else 2
                    nk = 512 // maps
                    if u >= 2:
                        pe.wait_ge(exp_done, u - 1 if u - 2 < base or l == 0 else base + 2 * (u - 1 - base))
                    mask = cb[:, CB[{"fox": "fox", "diff": "chunk", "swa": "chunk" if tile == 0 else "swa"}[kind] + str(tile)]]
                    o = ps_o[:, u % 2, :].rearrange("p (m k) -> p m k", m=maps)
                    pe.matmul(o, ident_b, mask.unsqueeze(1).to_broadcast([P, maps, nk]), start=True, stop=False,
                              skip_group_check=True)
                    jobs = [(h, j) for h in heads for j in range(2 if kind == "diff" else 1)]
                    for m, (h, j) in enumerate(jobs):
                        q, kk = operands(kind, h, j)
                        if kind == "fox":
                            pe.matmul(o[:, m, :], station_f[:, h, tile * P:(tile + 1) * P], moving_f[:, 0:nk],
                                      start=False, stop=False, skip_group_check=True)
                        ins = pe.matmul(o[:, m, :], q[:, tile * P:(tile + 1) * P], kk[:, 0:nk], start=False,
                                        stop=(m == maps - 1), skip_group_check=True)
                    ins.then_inc(logits_done, 1)

                def turn_probs(k):
                    kind, tile, heads = units[k]
                    u = base + k
                    if kind == "diff":
                        pe.wait_ge(probs_ready, k - 5)
                        src, blocks = pr[:, u % 2, :], 2
                    else:
                        pe.wait_ge(exp_done, u + 1 if l == 0 else base + 2 * (k + 1))
                        src, blocks = ex[:, u % 2, :], 4
                    if u >= 2:
                        pe.wait_ge(p_t_ready, u - 1)
                    for b in range(blocks):
                        ins = pe.transpose(ps_o[:, 2 + u % 2, b * P:(b + 1) * P], src[:, b * P:(b + 1) * P], ident)
                    ins.then_inc(p_turned, 1)

                def values(k):
                    kind, tile, heads = units[k]
                    u, kbs = base + k, tile + 1
                    pe.wait_ge(p_t_ready, u + 1)
                    if u >= 2:
                        pe.wait_ge(pv_out, u - 1)
                    dv = P if kind == "diff" else HD
                    for m, h in enumerate(heads):
                        for kb in range(kbs):
                            v = {"fox": v_n, "diff": vd_n, "swa": v_n}[kind]
                            at = (h // 4 if kind == "swa" else h) * dv
                            b = m * kbs + kb
                            ins = pe.matmul(ps_s[:, u % 2, m * dv:(m + 1) * dv], p_t[:, u % 2, b * P:(b + 1) * P],
                                            v[:, kb, at:at + dv], start=(kb == 0), stop=(kb == kbs - 1))
                    ins.then_inc(pv_done, 1)

                for k in range(len(units) + 2):
                    if k < len(units):
                        logits(k)
                    if 0 <= k - 1 < len(units):
                        turn_probs(k - 1)
                    if k >= 2:
                        values(k - 2)

            def scores(l):
                pe.wait_ge(keys_in, 16 * (l + 1))
                for tt in range(TT):
                    for k in range(HC):
                        b = k // 4
                        if tt == 1 and k % 4 == 0:
                            pe.wait_ge(scores_out, 8 * l + b + 1)
                        if tt == 0 and k % 2 == 0:
                            pe.wait_ge(pair_out, pair_index(l, "pq", k) + 1)
                        ins = pe.matmul(ps_o[:, b, (k % 4) * KEYS:(k % 4 + 1) * KEYS], pq_t[:, k, tt * P:(tt + 1) * P],
                                        keys[:, k, :], start=True, stop=True)
                        if k % 4 == 3:
                            ins.then_inc(scores_done, 1)

            def u_chunk(l, turn, i0, s):
                pe.wait_ge(lo_done, turn * RAW + START["u", l] + i0 + s + 1)
                if s % 2 == 0:
                    pe.wait_ge(pair_out, turn * 2 + (pair_index(l, "u", i0 + s) - 1))
                transposed_block(None, s)

            def scatter(l, half, turn, s):
                g0 = (2 * l + half) * HALF
                pe.wait_ge(hots_ready, turn * RAW + g0 + s + 1)
                if s % 2 == 0:
                    pe.wait_ge(gated, turn * 2 + g0 // 2 + s // 2 + 1)
                for k in range(TOK):
                    slot = s % 2 * TOK + k
                    ins = pe.matmul(ps_s[:, s // 2 % 2, slot * HALF:(slot + 1) * HALF], hot_j[:, slot, :],
                                    hot_i[:, slot, :], start=True, stop=True)
                ins.then_inc(hots_used, 1)

            def v_chunk(l, turn, i0, s):
                pe.wait_ge(lo_done, turn * RAW + START["v", l] + i0 + s + 1)
                pe.wait_ge(g_lo_done, turn * RAW + KEYS * l + i0 + s + 1)
                a = s % AHEAD
                for tt in range(TT):
                    t = slice(tt * P, (tt + 1) * P)
                    for g, w in ((g_hi, w_hi), (g_hi, w_lo), (g_lo, w_hi)):
                        for b in range(2):
                            ins = pe.matmul(ps_o[:, 2 * tt + b, :], g[:, a, t], w[:, a, b * 512:(b + 1) * 512],
                                            start=False, stop=False, skip_group_check=True)
                ins.then_inc(chunk_used, 1)

            pe.wait_ge(loads, 16 * N_LOADS)
            for l in range(DEPTH):
                turn_rows(turn_of["in", l], y, TT * turn_of["in", l] + TT)
                pe.wait_ge(h_ready, 2 * turn_of["in", l] + 2)
                if l == 0:
                    pe.wait_ge(late_in, 64)
                    for c in range(C):
                        ins = pe.matmul(ps_s[:, 0, 0:T], wf_s[:, c, :], hf[:, c, :], start=(c == 0), stop=(c == C - 1))
                    ins.then_inc(f_done, 1)
                    segment(l, "in", AB_BLOCKS, "T" * 8 + "R" * 16)
                else:
                    segment(l, "in", C_BLOCKS, "R" * 12)
                turn_queries(l)
                if l == 0:
                    pe.wait_ge(masks_ready, 1)
                    pe.wait_ge(f_ready, 1)
                pe.wait_ge(qk_ready, 9 if l else 4)
                pe.wait_ge(pair_out, pair_index(l, "out"))
                attention(l)
                turn_rows(turn_of["out", l], mix, TT * turn_of["out", l] + TT)
                pe.wait_ge(h_ready, 2 * turn_of["out", l] + 2)
                segment(l, "out", OUT_BLOCKS, "R" * 8)
                turn_rows(turn_of["pq", l], y, TT * turn_of["pq", l] + TT)
                pe.wait_ge(h_ready, 2 * turn_of["pq", l] + 2)
                segment(l, "pq", PQ_BLOCKS, "T" * 16)
                scores(l)
                with pe.Fori(0, TURNS) as turn:
                    for s in range(RAW):
                        u_chunk(l, turn, 0, s)
                pe.wait_ge(picks_ready, l + 1)
                for q in range(3):
                    for tt in range(TT):
                        ins = pe.transpose(ps_s[:, q // 2, (q % 2) * T + tt * P:(q % 2) * T + (tt + 1) * P], pk[:, q, tt, :], ident)
                ins.then_inc(picks_turned, 1)
                with pe.Fori(0, TURNS) as turn:
                    for s in range(RAW):
                        u_chunk(l, turn, HALF, s)
                        scatter(l, 0, turn, s)
                for b in range(4):
                    pe.matmul(ps_o[:, b, 0:P], ident_b, cb[:, CB["fox1"]][:, 0:P], start=True, stop=False,
                              skip_group_check=True)
                with pe.Fori(0, TURNS) as turn:
                    for s in range(RAW):
                        v_chunk(l, turn, 0, s)
                        scatter(l, 1, turn, s)
                with pe.Fori(0, TURNS) as turn:
                    for s in range(RAW):
                        v_chunk(l, turn, HALF, s)


SWA_ORDER = [4 * (2 * (s // 8) + s % 2) + s % 8 // 2 for s in range(SWA_HEADS)]


def by_blocks(w):
    k, n = w.shape
    return np.ascontiguousarray(w.reshape(k // P, P, n // P, P).transpose(2, 1, 0, 3)).reshape(n // P, P, k)


def laid_out(x, norm_mix, norm_ffn, norm_final, ab_w_in, ab_f_bias, ab_lambda, ab_subln, ab_w_out, c_w_in, c_sinks,
             c_w_out, peer_w_q, peer_sub_keys, peer_u, peer_v):
    a = {k: np.asarray(v) for k, v in locals().items()}
    fox = FOX_HEADS * HD
    w = a["ab_w_in"][0]
    cut = 3 * fox + FOX_HEADS
    w_c = a["c_w_in"][0]
    w_c_q = w_c[:, :SWA_HEADS * HD].reshape(D, SWA_HEADS, HD)[:, SWA_ORDER].reshape(D, SWA_HEADS * HD)
    gains = np.stack([a["norm_mix"][0], a["norm_ffn"][0], a["norm_mix"][1], a["norm_ffn"][1]])
    return [
        ("x", a["x"].reshape(T, D)),
        ("gains", gains.reshape(2 * DEPTH, C, P).transpose(2, 0, 1)),
        ("gain_final", a["norm_final"]),
        ("consts", float_constants()),
        ("masks", mask_constants()),
        ("w_ab", by_blocks(np.concatenate([w[:, :3 * fox], w[:, cut:]], axis=1))),
        ("w_f", w[:, 3 * fox:cut].reshape(C, P, FOX_HEADS).transpose(1, 0, 2)),
        ("f_bias", a["ab_f_bias"].reshape(FOX_HEADS, 1)),
        ("lam_vecs", a["ab_lambda"][0]),
        ("subln", a["ab_subln"][0]),
        ("w_ab_out", by_blocks(a["ab_w_out"][0])),
        ("w_c", by_blocks(np.concatenate([w_c_q, w_c[:, SWA_HEADS * HD:]], axis=1))),
        ("sinks", a["c_sinks"][0]),
        ("w_c_out", by_blocks(a["c_w_out"][0])),
        ("w_pq", np.stack([by_blocks(a["peer_w_q"][l]) for l in range(DEPTH)])),
        ("keys_t", a["peer_sub_keys"].reshape(DEPTH, HC, KEYS, P).transpose(0, 3, 1, 2)),
        ("u_t", a["peer_u"].reshape(DEPTH, KEYS, KEYS, C, P).transpose(0, 1, 4, 3, 2).reshape(DEPTH, KEYS, P, D)),
        ("v_e", a["peer_v"].reshape(DEPTH, KEYS, P, D)),
    ]


def kernel(**inputs):
    import concourse.bacc as bacc
    from concourse.bass_utils import run_bass_kernel_spmd

    nc = bacc.Bacc("TRN2", target_bir_lowering=False, num_devices=1)
    arrays, args = {}, []
    for name, a in laid_out(**inputs):
        a = np.ascontiguousarray(a)
        arrays[f"in_{name}"] = a
        args.append(nc.dram_tensor(f"in_{name}", a.shape, mybir.dt.from_np(a.dtype), kind="ExternalInput").ap())
    args.append(nc.dram_tensor("out_trunk", (T, D), F32, kind="ExternalOutput").ap())
    trunk(nc, *args)
    r = run_bass_kernel_spmd(nc, [arrays], core_ids=[0])
    return r.results[0]["out_trunk"].reshape(1, T, D)
```

```python
from contextlib import ExitStack

import concourse.bass as bass
import numpy as np
from concourse import mybir

F32 = mybir.dt.float32
F32R = mybir.dt.float32r
BF16 = mybir.dt.bfloat16
U32 = mybir.dt.uint32
ALU = mybir.AluOpType
ACT = mybir.ActivationFunctionType
AX_X = mybir.AxisListType.X

P = 128
D = 1024
C = D // P
T = 256
TT = T // P
DEPTH = 2
CHUNK = 64
HD = 64
ROT = HD // 4
THETA = 500000.0
EPS = 1e-6
FOX_HEADS = 8
DIFF_HEADS = 4
LAM_INIT = 0.2
SWA_HEADS = 16
PEER_HEADS = 8
HC = 2 * PEER_HEADS
KEYS = 128
TOPK = 16
NEG = -1e30
REPLACED = -3e38

AB_BLOCKS, C_BLOCKS, OUT_BLOCKS, PQ_BLOCKS = 24, 12, 8, HC
SEGMENTS = [("in", AB_BLOCKS), ("out", OUT_BLOCKS), ("pq", PQ_BLOCKS), ("u", KEYS), ("v", KEYS)]
START = {}
_at = 0
for _l in range(DEPTH):
    for _name, _count in SEGMENTS:
        START[_name, _l] = _at
        _at += (C_BLOCKS if _l else AB_BLOCKS) if _name == "in" else _count
CHUNKS = _at
RAW = 4
AHEAD = 2
SPLIT = D // 2
HALF = KEYS // 2
TOK = 8
GROUPS = T // TOK
PARTS = 3
TURNS = HALF // RAW
EARLY = 12
EXP_TURN = 10
TURN_PICKS = 13

CF = {}
_at = 0
for _name, _count in [("ident", P), ("iota", P), ("cos", TT * ROT // 2), ("sin", TT * ROT // 2),
                      ("mv_scale", 1), ("mv_add", 1), ("st_scale", FOX_HEADS), ("st_add", FOX_HEADS)]:
    CF[_name] = slice(_at, _at + _count)
    _at += _count
CF_COLS = _at
CB = {}
_at = 0
for _name, _count in [("ident", P), ("fox0", P), ("fox1", T), ("chunk0", P), ("chunk1", T), ("swa1", T)]:
    CB[_name] = slice(_at, _at + _count)
    _at += _count
CB_COLS = _at


def float_constants():
    c = np.zeros((P, CF_COLS), np.float32)
    c[:, CF["ident"]] = np.eye(P)
    c[:, CF["iota"]] = np.arange(P)
    inv = (1.0 / (np.float32(THETA) ** (np.arange(0, ROT, 2, dtype=np.float32) / np.float32(ROT)))).astype(np.float32)
    angle = (np.arange(T, dtype=np.float32)[:, None] * inv[None, :]).astype(np.float32)
    for name, f in (("cos", np.cos), ("sin", np.sin)):
        c[:, CF[name]] = f(angle).astype(np.float32).reshape(TT, P, ROT // 2).transpose(1, 0, 2).reshape(P, -1)
    c[0:8, CF["mv_scale"]] = -8.0
    c[32:40, CF["mv_add"]] = 1.0
    for h in range(FOX_HEADS):
        c[h, CF["st_add"].start + h] = 1.0
        c[32 + h, CF["st_scale"].start + h] = 8.0
    return c


def mask_constants():
    c = np.zeros((P, CB_COLS), np.float32)
    q, k = np.arange(P)[:, None], np.arange(T)[None, :]
    c[:, CB["ident"]] = np.eye(P)
    c[:, CB["fox0"]] = np.where(k[:, :P] <= q, 0, NEG)
    c[:, CB["fox1"]] = np.where(k <= q + P, 0, NEG)
    c[:, CB["chunk0"]] = np.where(k[:, :P] // CHUNK <= q // CHUNK, 0, NEG)
    c[:, CB["chunk1"]] = np.where(k // CHUNK <= (q + P) // CHUNK, 0, NEG)
    away = (q + P) // CHUNK - k // CHUNK
    c[:, CB["swa1"]] = np.where((away >= 0) & (away <= 1), 0, NEG)
    return c


def attention_units(l):
    if l == 0:
        out = [("fox", 0, range(4)), ("fox", 0, range(4, 8))]
        out += [("fox", 1, range(h, h + 2)) for h in range(0, 8, 2)]
        out += [("diff", 0, range(h, h + 2)) for h in (0, 2)]
        out += [("diff", 1, range(h, h + 1)) for h in range(DIFF_HEADS)]
        return out
    out = [("swa", 0, range(h, h + 4)) for h in range(0, SWA_HEADS, 4)]
    return out + [("swa", 1, range(h, h + 2)) for h in range(0, SWA_HEADS, 2)]


UNITS = [attention_units(0), attention_units(1)]


def trunk(nc, x, gains, gain_final, consts, masks, w_ab, w_f, f_bias, lam_vecs, subln, w_ab_out, w_c, sinks,
          w_c_out, w_pq, keys_t, u_t, v_e, out):
    with ExitStack() as ctx:
        def sb(name, shape, dt=F32):
            return ctx.enter_context(nc.sbuf_tensor(name, shape, dt))

        def psum(name, shape, dt=F32):
            return ctx.enter_context(nc.psum_tensor(name, shape, dt))

        def sem(name):
            return ctx.enter_context(nc.semaphore(name))

        xs = sb("xs", [P, TT, D])
        act = sb("act", [P, KEYS * T])
        h_hi = sb("h_hi", [P, C, T], F32R)
        h_lo = sb("h_lo", [P, C, T], F32R)
        raw = sb("raw", [P, RAW, D])
        w_hi = sb("w_hi", [P, AHEAD, D], F32R)
        w_lo = sb("w_lo", [P, AHEAD, D], F32R)
        g_hi = sb("g_hi", [P, AHEAD, T], F32R)
        g_lo = sb("g_lo", [P, AHEAD, T], F32R)
        eq_i = sb("eq_i", [P, HALF, TOK], BF16)
        hot_i = sb("hot_i", [P, 2, PARTS, HALF, TOK], BF16)
        hot_j = sb("hot_j", [P, 2, KEYS, TOK], BF16)
        iota_t = sb("iota_t", [P, KEYS, TOK], BF16)
        picks = sb("picks", [P, 2, T], BF16)
        w_parts = sb("w_parts", [P, PARTS, T], BF16)
        cf = sb("cf", [P, CF_COLS])
        cb = sb("cb", [P, CB_COLS], BF16)
        gain = sb("gain", [P, 2 * DEPTH, C])
        sink = sb("sink", [P, SWA_HEADS])
        neg_sink = sb("neg_sink", [P, SWA_HEADS])
        lamc = sb("lamc", [P, 2])
        bias_f = sb("bias_f", [P, 1])
        ms = sb("ms", [P, 8])
        root = sb("root", [P, 8])
        rstd = sb("rstd", [P, 8])
        newton = sb("newton", [P, 8])
        neg_max = sb("neg_max", [P, 2, 4])
        den = sb("den", [P, 4, 4])
        rden = sb("rden", [P, 4, 4])
        sink_e = sb("sink_e", [P, 4, 4])
        lsum = sb("lsum", [P, 2])

        def scratch(at, *shape, dt=F32):
            size = int(np.prod(shape))
            v = act[:, at:at + size]
            if dt != F32:
                v = v.bitcast(dt)
            names = "abcd"[:len(shape)]
            if len(shape) > 1:
                v = v.rearrange(f"p ({' '.join(names)}) -> p {' '.join(names)}",
                                **{n: s for n, s in zip(names[1:], shape[1:])})
            return v

        hf = scratch(0, C, T)
        y = scratch(2048, TT, D)
        pq_t = scratch(4096, HC, T)
        keys = scratch(8192, HC, KEYS)
        mix = scratch(10240, TT, D)
        g_fin = scratch(12288, D)
        lam_s = scratch(13312, 4, HD)
        lam_p = scratch(13568, 2, HD)
        sub_g = scratch(13696, P)
        cum = scratch(13824, T)
        ones = scratch(14080, T)
        moving_f = scratch(14336, T)
        fz = scratch(14592, T)
        fa = scratch(14848, T)
        fe = scratch(15104, T)
        fl = scratch(15360, T)
        wf_s = scratch(8192 - D, C, P)
        station_f = scratch(4096, FOX_HEADS, T)
        vd_n = scratch(6144, TT, 512)
        H2 = HALF * T
        k_pad = scratch(H2, 2, 8, T)
        v_n = scratch(H2 + 4096, TT, 512)
        qk_n = scratch(H2 + 5120, TT, 20 * HD)
        q_t = scratch(H2 + 7680, 8, T)
        fox_q = scratch(H2 + 9728, 4, T)
        ex = scratch(H2 + 10752, 2, 512)
        pr = scratch(H2 + 11776, 2, 256)
        p_t = scratch(H2 + 12288, 2, 512)
        rope_c = scratch(H2 + 13312, 20, 2, ROT // 2)
        rope_s = scratch(H2 + 13632, 20, 2, ROT // 2)
        dsq = scratch(H2 + 13952, TT, DIFF_HEADS, P)
        cb_in = scratch(H2 + 14976, CB_COLS)
        sc = scratch(H2, TT, HC, KEYS)
        sc2 = scratch(H2 + 4096, 2, KEYS)
        cand = scratch(H2 + 4352, 2, TOPK, TOPK)
        cand2 = scratch(H2 + 4864, 2, TOPK * TOPK)
        sv = scratch(H2 + 5376, TT, HC, TOPK)
        si = scratch(H2 + 5888, TT, HC, TOPK, dt=U32)
        sif = scratch(H2 + 6400, TT, HC, TOPK)
        tv = scratch(H2 + 6912, TT, P)
        tp = scratch(H2 + 7168, TT, P, dt=U32)
        ab_u = scratch(H2 + 7424, 2, TT * P, dt=U32)
        ab_f = scratch(H2 + 7936, 2, TT, P)
        tsum = scratch(H2 + 8448, TT * PEER_HEADS)
        pk = scratch(H2 + 8512, 3, TT, P)
        eq = scratch(H2 + 9280, P, TOPK)
        w_rest = scratch(H2 + 11328, 2, T)

        ps_a = psum("ps_a", [P, 2, 512])
        ps_o = psum("ps_o", [P, 4, 512])
        ps_s = psum("ps_s", [P, 2, 512])

        ident = cf[:, CF["ident"]]
        iota = cf[:, CF["iota"]]
        ident_b = cb[:, CB["ident"]]

        raw_full = [sem(f"raw_full{s}") for s in range(RAW)]
        hi_done = sem("hi_done")
        lo_done = sem("lo_done")
        chunk_used = sem("chunk_used")
        pair_out = sem("pair_out")
        loads = sem("loads")
        keys_in = sem("keys_in")
        masks_ready = sem("masks_ready")
        late_in = sem("late_in")
        zeroed = sem("zeroed")
        x_in = sem("x_in")
        x_new = sem("x_new")
        sq_done = sem("sq_done")
        ms_ready = sem("ms_ready")
        root_done = sem("root_done")
        y_ready = sem("y_ready")
        turned = sem("turned")
        hf_ready = sem("hf_ready")
        h_hi_done = sem("h_hi_done")
        h_ready = sem("h_ready")
        f_done = sem("f_done")
        f_abs = sem("f_abs")
        f_exp = sem("f_exp")
        f_ln = sem("f_ln")
        f_ready = sem("f_ready")
        lam_ready = sem("lam_ready")
        lam_exp = sem("lam_exp")
        roped = sem("roped")
        qk_turned = sem("qk_turned")
        qk_ready = sem("qk_ready")
        logits_done = sem("logits_done")
        max_done = sem("max_done")
        exp_done = sem("exp_done")
        probs_ready = sem("probs_ready")
        p_turned = sem("p_turned")
        p_t_ready = sem("p_t_ready")
        pv_done = sem("pv_done")
        pv_out = sem("pv_out")
        scores_done = sem("scores_done")
        scores_out = sem("scores_out")
        top_sub = sem("top_sub")
        top_exp = sem("top_exp")
        picks_ready = sem("picks_ready")
        picks_turned = sem("picks_turned")
        eq_ready = sem("eq_ready")
        hots_ready = sem("hots_ready")
        hots_used = sem("hots_used")
        gated = sem("gated")
        g_hi_done = sem("g_hi_done")
        g_lo_done = sem("g_lo_done")
        y_out = sem("y_out")
        stored = sem("stored")
        dve_step = sem("dve_step")
        act_step = sem("act_step")

        N_LOADS = 6
        norm_of = {("in", l): 2 * l for l in range(DEPTH)} | {("pq", l): 2 * l + 1 for l in range(DEPTH)}
        turn_of = {(s, l): 3 * l + k for l in range(DEPTH) for k, s in enumerate(("in", "out", "pq"))}

        def pair_index(l, seg, k=0):
            return (START[seg, l] - l * KEYS + k) // 2

        def ps_block(k):
            return ps_a[:, k % 4 // 2, (k % 2) * T:(k % 2 + 1) * T]

        block = ctx.enter_context(nc.Block())

        @block.sync
        def _(sp):
            for tt in range(TT):
                sp.dma_start(xs[:, tt, :], x[tt * P:(tt + 1) * P, :]).then_inc(x_in, 16)

            def load(n, src):
                if not isinstance(n, int) or n >= RAW:
                    sp.wait_ge(lo_done, n * 2 - 2 * (RAW - 1))
                sp.dma_start(raw[:, slot, :], src).then_inc(raw_full[slot], 16)

            for l in range(DEPTH):
                for seg, w in (("in", w_c if l else w_ab), ("out", w_c_out if l else w_ab_out), ("pq", w_pq[l])):
                    for k in range(w.shape[0]):
                        slot = k % RAW
                        load(START[seg, l] + k, w[k])
                for seg, w in (("u", u_t[l]), ("v", v_e[l])):
                    with sp.Fori(0, KEYS // RAW) as turn:
                        for slot in range(RAW):
                            load(turn * RAW + START[seg, l] + slot, w[bass.ds(turn * RAW + slot, 1)].rearrange("a p n -> (a p) n"))
            for tt in range(TT):
                sp.wait_ge(y_out, tt + 1)
                sp.dma_start(out[tt * P:(tt + 1) * P, :], y[:, tt, :]).then_inc(stored, 16)
            sp.wait_ge(stored, 16 * TT)

        @block.gpsimd
        def _(pool):
            pool.dma_start(cf[:], consts).then_inc(loads, 16)
            pool.dma_start(cb_in, masks).then_inc(loads, 16)
            pool.dma_start(gain[:], gains).then_inc(loads, 16)
            pool.dma_start(sink[:], sinks.partition_broadcast(P)).then_inc(loads, 16)
            pool.dma_start(lam_s, lam_vecs.partition_broadcast(P)).then_inc(loads, 16)
            pool.dma_start(sub_g, subln.partition_broadcast(P)).then_inc(loads, 16)
            pool.dma_start(keys, keys_t[0]).then_inc(keys_in, 16)
            pool.memset(wf_s, 0.0).then_inc(zeroed, 1)
            pool.memset(bias_f[:], 0.0).then_inc(zeroed, 1)
            pool.memset(ones, 1.0).then_inc(zeroed, 1)
            pool.memset(k_pad, 0.0).then_inc(zeroed, 1)
            pool.wait_ge(zeroed, 4)
            for r in (0, 32):
                pool.dma_start(wf_s[:, :, r:r + FOX_HEADS], w_f).then_inc(late_in, 16)
                pool.dma_start(bias_f[r:r + FOX_HEADS, :], f_bias).then_inc(late_in, 16)
            pool.memset(newton[:], 0.0).then_inc(hots_used, 2)
            pool.memset(root[:], 0.0).then_inc(gated, 2)
            pool.wait_ge(x_new, 8)
            pool.dma_start(keys, keys_t[1]).then_inc(keys_in, 16)
            pool.memset(k_pad, 0.0).then_inc(zeroed, 1)
            pool.wait_ge(x_new, 16)
            pool.dma_start(g_fin, gain_final.partition_broadcast(P)).then_inc(late_in, 16)

        @block.scalar
        def _(sc_e):
            steps = [0]

            def link(ins):
                steps[0] += 1
                ins.then_inc(act_step, 1)
                sc_e.wait_ge(act_step, steps[0])

            def split_hi(n, slot, waits_used=True):
                if isinstance(n, int):
                    if n >= CHUNKS:
                        return
                    sc_e.wait_ge(raw_full[slot % RAW], 16 * (n // RAW + 1))
                for half in range(2):
                    if waits_used:
                        sc_e.wait_ge(chunk_used, n * 2 - 2 * AHEAD + half + 1)
                    cols = slice(half * SPLIT, (half + 1) * SPLIT)
                    sc_e.activation(w_hi[:, slot % AHEAD, cols], raw[:, slot % RAW, cols], ACT.Copy).then_inc(hi_done, 1)

            def split_hi_in_loop(n, turn, ahead_of, s):
                sc_e.wait_ge(raw_full[(s + AHEAD) % RAW], turn * 16 + 16 * ((ahead_of + AHEAD) // RAW + 1))
                split_hi(n + AHEAD, s + AHEAD)

            def norm_squares(k):
                if k:
                    sc_e.wait_ge(x_new, 4 * k)
                else:
                    sc_e.wait_ge(x_in, 16 * TT)
                for tt in range(TT):
                    sc_e.activation(y[:, tt, :], xs[:, tt, :], ACT.Square, accum_out=rstd[:, tt:tt + 1]).then_inc(sq_done, 1)
                sc_e.wait_ge(ms_ready, MS_VALUE[k])
                sc_e.activation(root[:, 0:TT], ms[:, 0:TT], ACT.Sqrt).then_inc(root_done, 1)

            MS_VALUE = [1, 3, 4, 5, 6]

            def operand_hi(s):
                for half in range(2):
                    sc_e.wait_ge(hf_ready, 4 * s + 2 * half + 2)
                    c = slice(4 * half, 4 * half + 4)
                    sc_e.activation(h_hi[:, c, :], hf[:, c, :], ACT.Copy).then_inc(h_hi_done, 1)

            def turned_out(l, count):
                for b in range(count):
                    sc_e.wait_ge(qk_turned, 4 * l + b + 1)
                    two = ps_o[:, b % 4, :].rearrange("p (b t) -> p b t", b=2)
                    if b < count - (1 if l else 2):
                        sc_e.activation(q_t[:, 2 * b:2 * b + 2, :], two, ACT.Copy).then_inc(qk_ready, 1)
                    else:
                        keys_out(0 if l else 2 * b, two).then_inc(qk_ready, 1)

            def keys_out(at, two):
                sc_e.activation(k_pad[0:HD, 0, at:at + 2, :], two[0:HD], ACT.Copy)
                return sc_e.activation(k_pad[HD:P, 1, at:at + 2, :], two[HD:P], ACT.Copy)

            def pair(b):
                return ps_a[:, b % 2, :]

            def scores_to_rows(l, j):
                sc_e.wait_ge(scores_done, 8 * l + j + 1)
                sc_e.activation(sc[:, :, 2 * j:2 * j + 2, :], ps_o[:, j % 4, :].rearrange("p (t k e) -> p t k e", t=TT, k=2),
                                ACT.Copy).then_inc(scores_out, 1)

            def attention(l):
                base = len(UNITS[0]) * l
                for k, (kind, tile, heads) in enumerate(UNITS[l]):
                    u = base + k
                    maps = 4 if tile == 0 else 2
                    nk = 512 // maps
                    sc_e.wait_ge(max_done, u + 1)
                    if u >= 2:
                        sc_e.wait_ge(p_turned, u - 1)
                    if kind == "swa":
                        sc_e.activation(sink_e[:, u % 4, 0:maps], sink_e[:, u % 4, 0:maps], ACT.Exp).then_inc(exp_done, 1)
                    for m in range(maps):
                        ins = sc_e.activation(ex[:, u % 2, m * nk:(m + 1) * nk], ps_o[:, u % 2, m * nk:(m + 1) * nk],
                                              ACT.Exp, bias=neg_max[:, u % 2, m:m + 1], scale=HD ** -0.5,
                                              accum_out=den[:, u % 4, m:m + 1])
                    ins.then_inc(exp_done, 1)

            for n in range(AHEAD):
                split_hi(n, n, waits_used=False)
            for l in range(DEPTH):
                norm_squares(norm_of["in", l])
                operand_hi(turn_of["in", l])
                if l == 0:
                    sc_e.wait_ge(f_abs, 1)
                    sc_e.activation(fe, fa, ACT.Exp, scale=-1.0).then_inc(f_exp, 1)
                    sc_e.wait_ge(f_exp, 1)
                    sc_e.activation(fl, fe, ACT.Ln, bias=1.0).then_inc(f_ln, 1)
                    sc_e.wait_ge(lam_ready, 1)
                    sc_e.activation(lsum[:], lsum[:], ACT.Exp).then_inc(lam_exp, 1)
                sc_e.wait_ge(zeroed, 4 + l)
                blocks = C_BLOCKS if l else AB_BLOCKS
                for k in range(blocks):
                    n = START["in", l] + k
                    split_hi(n + AHEAD, k + AHEAD)
                    if k % 2:
                        sc_e.wait_ge(chunk_used, 2 * (n + 1))
                        b = k // 2
                        bank = pair(pair_index(l, "in", k - 1))
                        two = bank.rearrange("p (b t) -> p b t", b=2)
                        if l == 0 and b < 2:
                            sc_e.activation(fox_q[:, 2 * b:2 * b + 2, :], two, ACT.Copy).then_inc(pair_out, 1)
                        elif l == 0 and b < 4:
                            keys_out(2 * b - 4, two).then_inc(pair_out, 1)
                        else:
                            to, first = ([None] * 4 + [(v_n, 4)] * 2 + [(qk_n, 6)] * 4 + [(vd_n, 10)] * 2 if l == 0 else
                                         [(qk_n, 0)] * 5 + [(v_n, 5)])[b]
                            sc_e.activation(to[:, :, (b - first) * T:(b - first + 1) * T],
                                            bank.rearrange("p (t c) -> p t c", t=TT), ACT.Copy).then_inc(pair_out, 1)
                turned_out(l, 5 if l else 4)
                attention(l)
                if l == 0:
                    sc_e.wait_ge(ms_ready, 2)
                    sc_e.activation(root[:], ms[:], ACT.Sqrt).then_inc(root_done, 1)
                operand_hi(turn_of["out", l])
                for k in range(OUT_BLOCKS):
                    split_hi(START["out", l] + k + AHEAD, k + AHEAD)
                norm_squares(norm_of["pq", l])
                operand_hi(turn_of["pq", l])
                for k in range(PQ_BLOCKS):
                    n = START["pq", l] + k
                    split_hi(n + AHEAD, k + AHEAD)
                    if k % 2:
                        sc_e.wait_ge(chunk_used, 2 * (n + 1))
                        sc_e.activation(pq_t[:, k - 1:k + 1, :],
                                        pair(pair_index(l, "pq", k - 1)).rearrange("p (b t) -> p b t", b=2), ACT.Copy)\
                            .then_inc(pair_out, 1)
                        if k > 1:
                            scores_to_rows(l, k // 2 - 1)
                scores_to_rows(l, HC // 2 - 1)

                def u_chunks(turn, i0):
                    for s in range(RAW):
                        n0 = START["u", l] + i0 + s
                        split_hi_in_loop(turn * RAW + n0, turn, n0, s)
                        if s % 2:
                            at = turn * (RAW * T) + (i0 + s - 1) * T
                            sc_e.activation(act[:, bass.ds(at, 2 * T)], ps_a[:, s // 2, :], ACT.Gelu_apprx_tanh)\
                                .then_inc(pair_out, 1)

                with sc_e.Fori(0, EXP_TURN) as turn:
                    u_chunks(turn, 0)
                sc_e.wait_ge(top_sub, l + 1)
                sc_e.activation(pk[:, 2], pk[:, 2], ACT.Exp).then_inc(top_exp, 1)
                with sc_e.Fori(0, TURNS - EXP_TURN) as turn:
                    u_chunks(turn, EXP_TURN * RAW)
                with sc_e.Fori(0, TURNS) as turn:
                    u_chunks(turn, HALF)

                def g_rounded(i, slot):
                    sc_e.activation(g_hi[:, slot, :], act[:, bass.ds(i * T, T)], ACT.Copy).then_inc(g_hi_done, 1)

                for half in range(2):
                    i0 = half * HALF
                    sc_e.wait_ge(gated, 2 + (2 * l + half + 1) * GROUPS)
                    sc_e.wait_ge(chunk_used, 2 * (START["v", l] + i0))
                    for s in range(AHEAD):
                        g_rounded(i0 + s, s)
                    with sc_e.Fori(0, TURNS - 1) as turn:
                        for s in range(RAW):
                            n0 = START["v", l] + i0 + s
                            split_hi_in_loop(turn * RAW + n0, turn, n0, s)
                            g_rounded(turn * RAW + (i0 + s + AHEAD), s % AHEAD)
                    for s in range(RAW):
                        i = i0 + HALF - RAW + s
                        split_hi(START["v", l] + i + AHEAD, i + AHEAD)
                        if s + AHEAD < RAW:
                            sc_e.wait_ge(chunk_used, 2 * (START["v", l] + i + 1))
                            g_rounded(i + AHEAD, s % AHEAD)
            norm_squares(4)

        @block.vector
        def _(dve):
            steps = [0]

            def link(ins):
                steps[0] += 1
                ins.then_inc(dve_step, 1)
                dve.wait_ge(dve_step, steps[0])

            def rest_lo(n, slot, pieces=2):
                if isinstance(n, int) and n >= CHUNKS:
                    return
                count = 2 // pieces
                for piece in range(pieces):
                    dve.wait_ge(hi_done, n * 2 + (piece + 1) * count)
                    cols = slice(piece * count * SPLIT, (piece + 1) * count * SPLIT)
                    dve.tensor_tensor(w_lo[:, slot % AHEAD, cols], raw[:, slot % RAW, cols],
                                      w_hi[:, slot % AHEAD, cols].bitcast(F32), ALU.subtract).then_inc(lo_done, count)

            def inverse_root(n, count):
                dve.wait_ge(root_done, n)
                r, m, t = rstd[:, 0:count], ms[:, 0:count], newton[:, 0:count]
                link(dve.reciprocal(r, root[:, 0:count]))
                link(dve.tensor_tensor(t, r, r, ALU.mult))
                link(dve.tensor_tensor(t, t, m, ALU.mult))
                link(dve.tensor_scalar(t, t, -0.5, 1.5, ALU.mult, ALU.add))
                link(dve.tensor_tensor(r, r, t, ALU.mult))

            def norm_rows(k, n):
                dve.wait_ge(sq_done, TT * (k + 1))
                dve.tensor_scalar(ms[:, 0:TT], rstd[:, 0:TT], 1.0 / D, EPS, ALU.mult, ALU.add).then_inc(ms_ready, 1)
                inverse_root(n, TT)

            def operand(s, g=None):
                for b in range(4):
                    dve.wait_ge(turned, 4 * s + b + 1)
                    src = ps_o[:, b, :].rearrange("p (c t) -> p c t", c=2)
                    dst = hf[:, 2 * b:2 * b + 2, :]
                    if g is None:
                        dve.tensor_copy(dst, src).then_inc(hf_ready, 1)
                    else:
                        dve.tensor_tensor(dst, src, g[:, 2 * b:2 * b + 2].unsqueeze(2).to_broadcast([P, 2, T]),
                                          ALU.mult).then_inc(hf_ready, 1)
                for half in range(2):
                    dve.wait_ge(h_hi_done, 2 * s + half + 1)
                    c = slice(4 * half, 4 * half + 4)
                    dve.tensor_tensor(h_lo[:, c, :], hf[:, c, :], h_hi[:, c, :].bitcast(F32), ALU.subtract)\
                        .then_inc(h_ready, 1)

            def norm(k, n, s):
                norm_rows(k, n)
                for tt in range(TT):
                    dve.tensor_scalar(y[:, tt, :], xs[:, tt, :], rstd[:, tt:tt + 1], None, ALU.mult).then_inc(y_ready, 1)
                operand(s, gain[:, k, :])

            def fox_gates():
                dve.wait_ge(f_done, 1)
                dve.wait_ge(late_in, 64)
                link(dve.tensor_scalar(fz, ps_s[:, 0, 0:T], bias_f[:, 0:1], None, ALU.add))
                dve.scalar_tensor_tensor(out=fa, in0=fz, scalar=-1.0, in1=fz, op0=ALU.mult, op1=ALU.max).then_inc(f_abs, 1)
                dve.wait_ge(f_ln, 1)
                link(dve.scalar_tensor_tensor(out=fz, in0=fz, scalar=0.0, in1=fl, op0=ALU.min, op1=ALU.subtract))
                link(dve.tensor_tensor_scan(cum, ones, fz, 0.0, ALU.mult, ALU.add))
                dve.tensor_scalar(moving_f, cum, cf[:, CF["mv_scale"]], cf[:, CF["mv_add"]], ALU.mult, ALU.add)
                shape = [P, FOX_HEADS, T]
                link(dve.tensor_tensor(station_f, cum.unsqueeze(1).to_broadcast(shape),
                                       cf[:, CF["st_scale"]].unsqueeze(2).to_broadcast(shape), ALU.mult))
                dve.tensor_tensor(station_f, station_f, cf[:, CF["st_add"]].unsqueeze(2).to_broadcast(shape),
                                  ALU.add).then_inc(f_ready, 1)

            def lambda_row():
                dve.tensor_tensor(lam_p[:, 0, :], lam_s[:, 0, :], lam_s[:, 1, :], ALU.mult)
                link(dve.tensor_tensor(lam_p[:, 1, :], lam_s[:, 2, :], lam_s[:, 3, :], ALU.mult))
                dve.tensor_reduce(lsum[:], lam_p, AX_X, ALU.add).then_inc(lam_ready, 1)
                dve.wait_ge(lam_exp, 1)
                dve.memset(lamc[:, 0:1], 1.0)
                link(dve.tensor_tensor(lamc[:, 1:2], lsum[:, 1:2], lsum[:, 0:1], ALU.subtract))
                link(dve.tensor_scalar(lamc[:, 1:2], lamc[:, 1:2], -LAM_INIT, None, ALU.add))

            def rope(heads):
                for tt in range(TT):
                    both = qk_n[:, tt, 0:heads * HD].rearrange("p (h e) -> p h e", e=HD)[:, :, 0:ROT]
                    both = both.rearrange("p h (a r) -> p h a r", a=2)
                    shape = [P, heads, 2, ROT // 2]
                    for table, to in (("cos", rope_c), ("sin", rope_s)):
                        t = cf[:, CF[table]].rearrange("p (t r) -> p t r", t=TT)[:, tt, :]
                        ins = dve.tensor_tensor(to[:, 0:heads], both, t.unsqueeze(1).unsqueeze(1).to_broadcast(shape), ALU.mult)
                    link(ins)
                    dve.tensor_tensor(both[:, :, 0, :], rope_c[:, 0:heads, 0, :], rope_s[:, 0:heads, 1, :], ALU.subtract)
                    link(dve.tensor_tensor(both[:, :, 1, :], rope_c[:, 0:heads, 1, :], rope_s[:, 0:heads, 0, :], ALU.add))
                dve.sem_inc(roped, 1)

            def attention(l):
                base = len(UNITS[0]) * l
                units = UNITS[l]

                def exps(u):
                    return u + 1 if l == 0 else base + 2 * (u - base + 1)

                def maxima(k):
                    kind, tile, heads = units[k]
                    u, maps = base + k, 4 if tile == 0 else 2
                    dve.wait_ge(logits_done, u + 1)
                    m = neg_max[:, u % 2, 0:maps]
                    link(dve.tensor_reduce(m, ps_o[:, u % 2, :].rearrange("p (m k) -> p m k", m=maps), AX_X, ALU.max))
                    ins = dve.tensor_scalar(m, m, -HD ** -0.5, None, ALU.mult)
                    if kind == "swa":
                        h = slice(heads[0], heads[0] + maps)
                        link(ins)
                        link(dve.tensor_tensor(m, m, neg_sink[:, h], ALU.min))
                        ins = dve.tensor_tensor(sink_e[:, u % 4, 0:maps], sink[:, h], m, ALU.add)
                    ins.then_inc(max_done, 1)

                def inverses(k):
                    kind, tile, heads = units[k]
                    u, maps = base + k, 4 if tile == 0 else 2
                    dve.wait_ge(exp_done, exps(u))
                    d, r = den[:, u % 4, 0:maps], rden[:, u % 4, 0:maps]
                    if kind == "swa":
                        link(dve.tensor_tensor(d, d, sink_e[:, u % 4, 0:maps], ALU.add))
                    link(dve.reciprocal(r, d))
                    if kind == "diff":
                        n = maps // 2
                        r2 = r.rearrange("p (h j) -> p h j", j=2)
                        link(dve.tensor_tensor(r2, r2, lamc[:].unsqueeze(1).to_broadcast([P, n, 2]), ALU.mult))
                        e = ex[:, u % 2, :].rearrange("p (m k) -> p m k", m=maps)
                        link(dve.tensor_tensor(e, e, r.unsqueeze(2).to_broadcast([P, maps, 512 // maps]), ALU.mult))
                        e = ex[:, u % 2, :].rearrange("p (h j k) -> p h j k", j=2, h=n)
                        if u >= 2:
                            dve.wait_ge(p_turned, u - 1)
                        dve.tensor_tensor(pr[:, u % 2, :].rearrange("p (h k) -> p h k", h=n), e[:, :, 0], e[:, :, 1],
                                          ALU.add).then_inc(probs_ready, 1)

                def p_t_out(k):
                    kind, tile, heads = units[k]
                    u = base + k
                    w = 256 if kind == "diff" else 512
                    dve.wait_ge(p_turned, u + 1)
                    if u >= 2:
                        dve.wait_ge(pv_done, u - 1)
                    dve.tensor_copy(p_t[:, u % 2, 0:w], ps_o[:, 2 + u % 2, 0:w]).then_inc(p_t_ready, 1)

                def values_out(k):
                    kind, tile, heads = units[k]
                    u, n = base + k, len(heads)
                    dve.wait_ge(pv_done, u + 1)
                    if kind == "diff":
                        dst = mix[:, tile, 512 + heads[0] * P:512 + (heads[0] + n) * P]
                        dve.tensor_copy(dst, ps_s[:, u % 2, 0:n * P]).then_inc(pv_out, 1)
                    else:
                        dst = mix[:, tile, heads[0] * HD:(heads[0] + n) * HD].rearrange("p (m e) -> p m e", m=n)
                        dve.tensor_tensor(dst, ps_s[:, u % 2, 0:n * HD].rearrange("p (m e) -> p m e", m=n),
                                          rden[:, u % 4, 0:n].unsqueeze(2).to_broadcast([P, n, HD]), ALU.mult)\
                            .then_inc(pv_out, 1)

                for k in range(len(units) + 2):
                    if k < len(units):
                        maxima(k)
                    if 0 <= k - 1 < len(units):
                        inverses(k - 1)
                        p_t_out(k - 1)
                    if k >= 2:
                        values_out(k - 2)

            def diff_norm():
                dve.wait_ge(pv_out, len(UNITS[0]))
                o = mix[:, :, 512:1024].rearrange("p t (h e) -> p t h e", h=DIFF_HEADS)
                link(dve.tensor_tensor(dsq, o, o, ALU.mult))
                link(dve.tensor_reduce(ms[:].rearrange("p (t h) -> p t h", t=TT), dsq, AX_X, ALU.add))
                dve.tensor_scalar(ms[:], ms[:], 1.0 / P, EPS, ALU.mult, ALU.add).then_inc(ms_ready, 1)
                link(dve.tensor_scalar(sub_g, sub_g, 1.0 - LAM_INIT, None, ALU.mult))
                inverse_root(2, 8)
                r = rstd[:].rearrange("p (t h) -> p t h", t=TT)
                shape = [P, TT, DIFF_HEADS, P]
                link(dve.tensor_tensor(o, o, r.unsqueeze(3).to_broadcast(shape), ALU.mult))
                link(dve.tensor_tensor(o, o, sub_g.unsqueeze(1).unsqueeze(1).to_broadcast(shape), ALU.mult))

            def top16(values, indices, src, spare):
                link(dve.max(values[:, 0:8], src))
                dve.max_index(indices[:, 0:8], values[:, 0:8], src)
                link(dve.match_replace(spare, values[:, 0:8], src, REPLACED))
                link(dve.max(values[:, 8:16], spare))
                link(dve.max_index(indices[:, 8:16], values[:, 8:16], spare))

            def select(l, i):
                lists = TT * HC
                finals = TT * PEER_HEADS
                if i < lists:
                    h, tt, c = i // 4, i // 2 % 2, i % 2
                    k = 2 * h + c
                    dve.wait_ge(scores_out, 8 * l + h + 1)
                    top16(sv[:, tt, k, :], si[:, tt, k, :], sc[:, tt, k, :], sc2[:, i % 2, :])
                elif i < lists + finals:
                    tt, h = divmod(i - lists, PEER_HEADS)
                    shape = [P, TOPK, TOPK]
                    link(dve.tensor_tensor(cand[:, i % 2], sv[:, tt, 2 * h, :].unsqueeze(2).to_broadcast(shape),
                                           sv[:, tt, 2 * h + 1, :].unsqueeze(1).to_broadcast(shape), ALU.add))
                    top16(tv[:, tt, h * TOPK:(h + 1) * TOPK], tp[:, tt, h * TOPK:(h + 1) * TOPK],
                          cand[:, i % 2].rearrange("p a b -> p (a b)"), cand2[:, i % 2, :])
                elif i == lists + finals:
                    t = tv.rearrange("p t (h k) -> p (t h) k", k=TOPK)
                    w = pk[:, 2].rearrange("p t (h k) -> p (t h) k", k=TOPK)
                    dve.tensor_tensor(w, t, t[:, :, 0:1].to_broadcast([P, finals, TOPK]), ALU.subtract).then_inc(top_sub, 1)
                    flat = tp.rearrange("p t k -> p (t k)")
                    dve.tensor_scalar(ab_u[:, 0], flat, 4, None, ALU.logical_shift_right)
                    link(dve.tensor_scalar(ab_u[:, 1], flat, TOPK - 1, None, ALU.bitwise_and))
                    dve.tensor_copy(ab_f.rearrange("p s t k -> p s (t k)"), ab_u)
                    link(dve.tensor_copy(sif, si))
                elif i < lists + finals + 13:
                    which, step = divmod(i - lists - finals - 1, 3)
                    tt, side = divmod(which, 2)
                    if step == 0:
                        link(dve.tensor_tensor(eq, ab_f[:, side, tt, :].unsqueeze(2).to_broadcast([P, P, TOPK]),
                                               iota[:, 0:TOPK].unsqueeze(1).to_broadcast([P, P, TOPK]), ALU.is_equal))
                    elif step == 1:
                        e4 = eq.rearrange("p (h k) a -> p h k a", h=PEER_HEADS)
                        held = sif[:, tt].rearrange("p (h s) a -> p h s a", s=2)[:, :, side, :]
                        link(dve.tensor_tensor(e4, e4, held.unsqueeze(2).to_broadcast([P, PEER_HEADS, TOPK, TOPK]), ALU.mult))
                    else:
                        link(dve.tensor_reduce(pk[:, side, tt, :], eq, AX_X, ALU.add))
                elif i == lists + finals + 13:
                    dve.wait_ge(top_exp, l + 1)
                    w = pk[:, 2].rearrange("p t (h k) -> p (t h) k", k=TOPK)
                    link(dve.tensor_reduce(tsum, w, AX_X, ALU.add))
                    link(dve.reciprocal(tsum, tsum))
                    dve.tensor_tensor(w, w, tsum.unsqueeze(2).to_broadcast([P, finals, TOPK]), ALU.mult).then_inc(picks_ready, 1)

            def picks_to_parts(l):
                dve.wait_ge(picks_turned, l + 1)
                dve.wait_ge(hots_used, 2 * l * GROUPS + 2)
                dve.tensor_copy(picks[:], ps_s[:, 0, :].rearrange("p (s t) -> p s t", s=2))
                w = ps_s[:, 1, 0:T]
                link(dve.tensor_copy(w_parts[:, 0, :], w))
                link(dve.tensor_tensor(w_rest[:, 0, :], w, w_parts[:, 0, :], ALU.subtract))
                link(dve.tensor_copy(w_parts[:, 1, :], w_rest[:, 0, :]))
                link(dve.tensor_tensor(w_rest[:, 1, :], w_rest[:, 0, :], w_parts[:, 1, :], ALU.subtract))
                link(dve.tensor_copy(w_parts[:, 2, :], w_rest[:, 1, :]))

            def hots(half, g0, group, static):
                dve.wait_ge(hots_used, group + (g0 + 1))
                if not isinstance(group, int) or group or g0:
                    dve.wait_ge(hots_ready, group + g0)
                t = bass.ds(group * TOK, TOK)
                i_t = picks[:, 0, t].unsqueeze(1).to_broadcast([P, HALF, TOK])
                j_t = picks[:, 1, t].unsqueeze(1).to_broadcast([P, KEYS, TOK])
                dve.tensor_tensor(eq_i[:], iota_t[:, half * HALF:(half + 1) * HALF, :], i_t, ALU.is_equal).then_inc(eq_ready, 1)
                dve.tensor_tensor(hot_j[:, static], iota_t[:], j_t, ALU.is_equal)

                dve.wait_ge(eq_ready, group + (g0 + 1))
                shape = [P, PARTS, HALF, TOK]
                w = w_parts[:, :, bass.ds(group * TOK, TOK)].unsqueeze(2).to_broadcast(shape)
                dve.tensor_tensor(hot_i[:, static], eq_i[:].unsqueeze(1).to_broadcast(shape), w, ALU.mult).then_inc(hots_ready, 1)

            def gate(half, g0, group, static):
                dve.wait_ge(hots_used, group + (g0 + 3))
                a = act[:, half * HALF * T:(half + 1) * HALF * T].rearrange("p (i t) -> p i t", t=T)[:, :, bass.ds(group * TOK, TOK)]
                dve.tensor_tensor(a, a, ps_s[:, static, :].rearrange("p (t i) -> p i t", i=HALF), ALU.mult).then_inc(gated, 1)

            def scatter_turn(l, half, turn, n0, with_g, first=False, last=False):
                g0 = (2 * l + half) * GROUPS
                for s in range(RAW):
                    rest_lo(turn * RAW + (n0 + s + AHEAD), s + AHEAD)
                    if with_g and not (last and s + AHEAD >= RAW):
                        g_rest(l, turn * RAW + (s + AHEAD), s % AHEAD)
                    if s % 2 == 0 and not (first and s == 0):
                        gate(half, g0, turn * 2 + (s // 2 - 1), (s // 2 + 1) % 2)
                    if s % 2 == 1 and not (last and s == RAW - 1):
                        hots(half, g0, turn * 2 + (s // 2 + 1), (s // 2 + 1) % 2)

            def g_rest(l, i, slot):
                dve.wait_ge(g_hi_done, i + KEYS * l + 1)
                dve.tensor_tensor(g_lo[:, slot, :], act[:, bass.ds(i * T, T)], g_hi[:, slot, :].bitcast(F32), ALU.subtract)\
                    .then_inc(g_lo_done, 1)

            dve.wait_ge(loads, 16 * N_LOADS)
            dve.tensor_copy(cb[:], cb_in).then_inc(masks_ready, 1)
            dve.tensor_copy(iota_t[:], iota.unsqueeze(2).to_broadcast([P, KEYS, TOK]))
            dve.wait_ge(x_in, 16 * TT)
            dve.wait_ge(zeroed, 3)
            dve.wait_ge(hots_used, 2)
            dve.wait_ge(gated, 2)
            for n in range(AHEAD):
                rest_lo(n, n)
            roots = [0]

            def next_root():
                roots[0] += 1
                return roots[0]

            for l in range(DEPTH):
                norm(2 * l, next_root(), turn_of["in", l])
                if l == 0:
                    fox_gates()
                    lambda_row()
                    next_root()
                for k in range(C_BLOCKS if l else AB_BLOCKS):
                    rest_lo(START["in", l] + k + AHEAD, k + AHEAD)
                dve.wait_ge(pair_out, pair_index(l, "in") + (10 if l == 0 else 5))
                rope(20 if l else 16)
                if l == 1:
                    link(dve.tensor_scalar(neg_sink[:], sink[:], -1.0, None, ALU.mult))
                attention(l)
                if l == 0:
                    diff_norm()
                dve.wait_ge(pv_out, len(UNITS[0]) * (l + 1))
                dve.sem_inc(y_ready, TT)
                operand(turn_of["out", l])
                for k in range(OUT_BLOCKS):
                    n = START["out", l] + k
                    rest_lo(n + AHEAD, k + AHEAD)
                    if k % 2:
                        dve.wait_ge(chunk_used, 2 * (n + 1))
                        to = xs[:, :, (k - 1) * P:(k + 1) * P]
                        two = ps_a[:, pair_index(l, "out", k - 1) % 2, :].rearrange("p (t c) -> p t c", t=TT)
                        dve.tensor_tensor(to, to, two, ALU.add).then_inc(pair_out, 1)
                dve.wait_ge(pair_out, pair_index(l, "pq"))
                dve.sem_inc(x_new, 4)
                norm(2 * l + 1, next_root(), turn_of["pq", l])
                for k in range(PQ_BLOCKS):
                    rest_lo(START["pq", l] + k + AHEAD, k + AHEAD, pieces=2 if k < PQ_BLOCKS - EARLY else 1)
                    if k >= PQ_BLOCKS - EARLY:
                        select(l, k - (PQ_BLOCKS - EARLY))
                for i in range(HALF):
                    if i < (TURN_PICKS + 1) * RAW - 2:
                        select(l, EARLY + i)
                    elif i == (TURN_PICKS + 1) * RAW - 2:
                        picks_to_parts(l)
                    rest_lo(START["u", l] + i + AHEAD, i + AHEAD, pieces=1)
                for half in range(2):
                    n0 = START["u", l] + HALF if half == 0 else START["v", l]
                    g0 = (2 * l + half) * GROUPS
                    hots(half, g0, 0, 0)
                    if half == 1:
                        gate(0, g0 - GROUPS, GROUPS - 1, 1)
                        for s in range(AHEAD):
                            g_rest(l, s, s)
                    scatter_turn(l, half, 0, n0, half == 1, first=True)
                    with dve.Fori(1, TURNS - 1) as turn:
                        scatter_turn(l, half, turn, n0, half == 1)
                    scatter_turn(l, half, TURNS - 1, n0, half == 1, last=True)
                gate(1, (2 * l + 1) * GROUPS, GROUPS - 1, 1)
                for s in range(AHEAD):
                    g_rest(l, HALF + s, s)
                n0 = START["v", l] + HALF
                with dve.Fori(0, TURNS - 1) as turn:
                    for s in range(RAW):
                        rest_lo(turn * RAW + n0 + s + AHEAD, s + AHEAD)
                        g_rest(l, turn * RAW + HALF + s + AHEAD, s % AHEAD)
                for s in range(RAW):
                    rest_lo(n0 + HALF - RAW + s + AHEAD, s + AHEAD)
                    if s + AHEAD < RAW:
                        g_rest(l, KEYS - RAW + s + AHEAD, s)
                dve.wait_ge(chunk_used, 2 * (START["v", l] + KEYS))
                for b in range(4):
                    to = xs[:, b // 2, (b % 2) * 512:(b % 2 + 1) * 512]
                    dve.tensor_tensor(to, to, ps_o[:, b, :], ALU.add).then_inc(x_new, 1)
                dve.wait_ge(x_new, 8 * l + 8)
            norm_rows(4, next_root())
            dve.wait_ge(late_in, 80)
            for tt in range(TT):
                dve.scalar_tensor_tensor(out=y[:, tt, :], in0=xs[:, tt, :], scalar=rstd[:, tt:tt + 1], in1=g_fin,
                                         op0=ALU.mult, op1=ALU.mult).then_inc(y_out, 1)

        @block.tensor
        def _(pe):
            def transposed_block(n, k):
                o = ps_block(k)
                for c in range(C):
                    if c % (C // 2) == 0:
                        pe.wait_ge(lo_done, n * 2 + (2 * c // C + 1))
                    cols = slice(c * P, (c + 1) * P)
                    hi, lo = w_hi[:, k % AHEAD, cols], w_lo[:, k % AHEAD, cols]
                    pe.matmul(o, hi, h_hi[:, c, :], start=(c == 0), stop=False)
                    pe.matmul(o, hi, h_lo[:, c, :], start=False, stop=False)
                    ins = pe.matmul(o, lo, h_hi[:, c, :], start=False, stop=(c == C - 1))
                    if c % (C // 2) == C // 2 - 1:
                        ins.then_inc(chunk_used, 1)

            def row_chunk(n, k):
                for c in range(C // 2):
                    if c % 2 == 0:
                        pe.wait_ge(lo_done, 2 * n + c // 2 + 1)
                    cols = slice(c * T, (c + 1) * T)
                    hi, lo = w_hi[:, k % AHEAD, cols], w_lo[:, k % AHEAD, cols]
                    for tt in range(TT):
                        o = ps_a[:, k % 4 // 2, tt * T:(tt + 1) * T]
                        x_hi, x_lo = (h[:, k % 2 * (C // 2) + c, tt * P:(tt + 1) * P] for h in (h_hi, h_lo))
                        first = k % 2 == 0 and tt == 0 and c == 0
                        last = k % 2 == 1 and tt == TT - 1 and c == C // 2 - 1
                        pe.matmul(o, x_hi, hi, start=first, stop=False, skip_group_check=True)
                        pe.matmul(o, x_hi, lo, start=False, stop=False, skip_group_check=True)
                        ins = pe.matmul(o, x_lo, hi, start=False, stop=last, skip_group_check=True)
                    if c % 2:
                        ins.then_inc(chunk_used, 1)

            def turn_rows(s, src, count):
                pe.wait_ge(y_ready, count)
                for c in range(C):
                    for tt in range(TT):
                        ins = pe.transpose(ps_o[:, c // 2, (c % 2) * T + tt * P:(c % 2) * T + (tt + 1) * P],
                                           src[:, tt, c * P:(c + 1) * P], ident)
                    if c % 2:
                        ins.then_inc(turned, 1)

            def segment(l, seg, count, kinds):
                for k in range(count):
                    n = START[seg, l] + k
                    p = pair_index(l, seg, k)
                    if k % 2 == 0 and p >= 2:
                        pe.wait_ge(pair_out, p - 1)
                    (transposed_block if kinds[k] == "T" else row_chunk)(n, k)
                    if seg == "pq" and k % 2 and k > 1:
                        scores(l, k // 2 - 1)

            def turn_queries(l):
                pe.wait_ge(roped, l + 1)
                for b in range(10 if l else 8):
                    if b == 8:
                        pe.wait_ge(qk_ready, 4 * l + 1)
                    for tt in range(TT):
                        src = qk_n[:, tt, b * P:(b + 1) * P]
                        at = (b % 2) * T + tt * P
                        ins = pe.transpose(ps_o[:, b // 2 % 4, at:at + P], src, ident)
                    if b % 2:
                        ins.then_inc(qk_turned, 1)

            def attention(l):
                base = len(UNITS[0]) * l
                units = UNITS[l]

                def operands(kind, h, j):
                    if kind == "fox":
                        return fox_q[:, h // 2, :], k_pad[:, h % 2, h // 2, :]
                    if kind == "diff":
                        return q_t[:, h, :], k_pad[:, j, DIFF_HEADS + h, :]
                    g = h // 4
                    return q_t[:, h % 4 + 4 * (g // 2), :], k_pad[:, g % 2, g // 2, :]

                def logits(k):
                    kind, tile, heads = units[k]
                    u, maps = base + k, 4 if tile == 0 else 2
                    nk = 512 // maps
                    if u >= 2:
                        pe.wait_ge(exp_done, u - 1 if u - 2 < base or l == 0 else base + 2 * (u - 1 - base))
                    mask = cb[:, CB[{"fox": "fox", "diff": "chunk", "swa": "chunk" if tile == 0 else "swa"}[kind] + str(tile)]]
                    o = ps_o[:, u % 2, :].rearrange("p (m k) -> p m k", m=maps)
                    pe.matmul(o, ident_b, mask.unsqueeze(1).to_broadcast([P, maps, nk]), start=True, stop=False,
                              skip_group_check=True)
                    jobs = [(h, j) for h in heads for j in range(2 if kind == "diff" else 1)]
                    for m, (h, j) in enumerate(jobs):
                        q, kk = operands(kind, h, j)
                        if kind == "fox":
                            pe.matmul(o[:, m, :], station_f[:, h, tile * P:(tile + 1) * P], moving_f[:, 0:nk],
                                      start=False, stop=False, skip_group_check=True)
                        ins = pe.matmul(o[:, m, :], q[:, tile * P:(tile + 1) * P], kk[:, 0:nk], start=False,
                                        stop=(m == maps - 1), skip_group_check=True)
                    ins.then_inc(logits_done, 1)

                def turn_probs(k):
                    kind, tile, heads = units[k]
                    u = base + k
                    if kind == "diff":
                        pe.wait_ge(probs_ready, k - 5)
                        src, blocks = pr[:, u % 2, :], 2
                    else:
                        pe.wait_ge(exp_done, u + 1 if l == 0 else base + 2 * (k + 1))
                        src, blocks = ex[:, u % 2, :], 4
                    if u >= 2:
                        pe.wait_ge(p_t_ready, u - 1)
                    for b in range(blocks):
                        ins = pe.transpose(ps_o[:, 2 + u % 2, b * P:(b + 1) * P], src[:, b * P:(b + 1) * P], ident)
                    ins.then_inc(p_turned, 1)

                def values(k):
                    kind, tile, heads = units[k]
                    u, kbs = base + k, tile + 1
                    pe.wait_ge(p_t_ready, u + 1)
                    if u >= 2:
                        pe.wait_ge(pv_out, u - 1)
                    dv = P if kind == "diff" else HD
                    for m, h in enumerate(heads):
                        for kb in range(kbs):
                            v = {"fox": v_n, "diff": vd_n, "swa": v_n}[kind]
                            at = (h // 4 if kind == "swa" else h) * dv
                            b = m * kbs + kb
                            ins = pe.matmul(ps_s[:, u % 2, m * dv:(m + 1) * dv], p_t[:, u % 2, b * P:(b + 1) * P],
                                            v[:, kb, at:at + dv], start=(kb == 0), stop=(kb == kbs - 1))
                    ins.then_inc(pv_done, 1)

                for k in range(len(units) + 2):
                    if k < len(units):
                        logits(k)
                    if 0 <= k - 1 < len(units):
                        turn_probs(k - 1)
                    if k >= 2:
                        values(k - 2)

            def scores(l, j):
                pe.wait_ge(keys_in, 16 * (l + 1))
                pe.wait_ge(pair_out, pair_index(l, "pq", 2 * j) + 1)
                if j >= 4:
                    pe.wait_ge(scores_out, 8 * l + j - 3)
                for tt in range(TT):
                    for c in range(2):
                        at = (2 * tt + c) * KEYS
                        ins = pe.matmul(ps_o[:, j % 4, at:at + KEYS], pq_t[:, 2 * j + c, tt * P:(tt + 1) * P],
                                        keys[:, 2 * j + c, :], start=True, stop=True)
                ins.then_inc(scores_done, 1)

            def u_chunk(l, turn, i0, s):
                if s % 2 == 0:
                    pe.wait_ge(pair_out, turn * 2 + (pair_index(l, "u", i0 + s) - 1))
                transposed_block(turn * RAW + (START["u", l] + i0 + s), s)

            def scatter(l, half, turn, b):
                g0 = (2 * l + half) * GROUPS
                pe.wait_ge(hots_ready, turn * 2 + g0 + b + 1)
                pe.wait_ge(gated, turn * 2 + g0 + b + 1)
                for k in range(TOK):
                    for part in range(PARTS):
                        ins = pe.matmul(ps_s[:, b, k * HALF:(k + 1) * HALF], hot_j[:, b, :, k], hot_i[:, b, part, :, k],
                                        start=(part == 0), stop=(part == PARTS - 1))
                ins.then_inc(hots_used, 1)

            def v_chunk(l, turn, i0, s):
                pe.wait_ge(g_lo_done, turn * RAW + (KEYS * l + i0 + s + 1))
                a = s % AHEAD
                for b in range(2):
                    pe.wait_ge(lo_done, turn * (2 * RAW) + (2 * (START["v", l] + i0 + s) + b + 1))
                    cols = slice(b * SPLIT, (b + 1) * SPLIT)
                    for tt in range(TT):
                        t = slice(tt * P, (tt + 1) * P)
                        for g, w in ((g_hi, w_hi), (g_hi, w_lo), (g_lo, w_hi)):
                            ins = pe.matmul(ps_o[:, 2 * tt + b, :], g[:, a, t], w[:, a, cols],
                                            start=False, stop=False, skip_group_check=True)
                    ins.then_inc(chunk_used, 1)

            pe.wait_ge(loads, 16 * N_LOADS)
            for l in range(DEPTH):
                turn_rows(turn_of["in", l], y, TT * turn_of["in", l] + TT)
                pe.wait_ge(h_ready, 2 * turn_of["in", l] + 2)
                if l == 0:
                    pe.wait_ge(late_in, 64)
                    for c in range(C):
                        ins = pe.matmul(ps_s[:, 0, 0:T], wf_s[:, c, :], hf[:, c, :], start=(c == 0), stop=(c == C - 1))
                    ins.then_inc(f_done, 1)
                    segment(l, "in", AB_BLOCKS, "T" * 8 + "R" * 16)
                else:
                    segment(l, "in", C_BLOCKS, "R" * 12)
                turn_queries(l)
                if l == 0:
                    pe.wait_ge(masks_ready, 1)
                    pe.wait_ge(f_ready, 1)
                pe.wait_ge(qk_ready, 9 if l else 4)
                pe.wait_ge(pair_out, pair_index(l, "out"))
                attention(l)
                turn_rows(turn_of["out", l], mix, TT * turn_of["out", l] + TT)
                pe.wait_ge(h_ready, 2 * turn_of["out", l] + 2)
                segment(l, "out", OUT_BLOCKS, "R" * 8)
                turn_rows(turn_of["pq", l], y, TT * turn_of["pq", l] + TT)
                pe.wait_ge(h_ready, 2 * turn_of["pq", l] + 2)
                segment(l, "pq", PQ_BLOCKS, "T" * 16)
                scores(l, HC // 2 - 1)
                with pe.Fori(0, TURN_PICKS) as turn:
                    for s in range(RAW):
                        u_chunk(l, turn, 0, s)
                pe.wait_ge(picks_ready, l + 1)
                for q in range(3):
                    for tt in range(TT):
                        ins = pe.transpose(ps_s[:, q // 2, (q % 2) * T + tt * P:(q % 2) * T + (tt + 1) * P], pk[:, q, tt, :], ident)
                ins.then_inc(picks_turned, 1)
                with pe.Fori(0, TURNS - TURN_PICKS) as turn:
                    for s in range(RAW):
                        u_chunk(l, turn, TURN_PICKS * RAW, s)
                with pe.Fori(0, TURNS) as turn:
                    for s in range(RAW):
                        u_chunk(l, turn, HALF, s)
                        if s % 2:
                            scatter(l, 0, turn, s // 2)
                for b in range(4):
                    pe.matmul(ps_o[:, b, 0:P], ident_b, cb[:, CB["fox1"]][:, 0:P], start=True, stop=False,
                              skip_group_check=True)
                with pe.Fori(0, TURNS) as turn:
                    for s in range(RAW):
                        v_chunk(l, turn, 0, s)
                        if s % 2:
                            scatter(l, 1, turn, s // 2)
                with pe.Fori(0, TURNS) as turn:
                    for s in range(RAW):
                        v_chunk(l, turn, HALF, s)


SWA_ORDER = [4 * (2 * (s // 8) + s % 2) + s % 8 // 2 for s in range(SWA_HEADS)]


def by_blocks(w):
    k, n = w.shape
    return np.ascontiguousarray(w.reshape(k // P, P, n // P, P).transpose(2, 1, 0, 3)).reshape(n // P, P, k)


def by_row_chunks(w):
    k, n = w.shape
    return np.ascontiguousarray(w.reshape(2, k // T, P, n // T, T).transpose(3, 0, 2, 1, 4)).reshape(n // P, P, k)


def laid_out(x, norm_mix, norm_ffn, norm_final, ab_w_in, ab_f_bias, ab_lambda, ab_subln, ab_w_out, c_w_in, c_sinks,
             c_w_out, peer_w_q, peer_sub_keys, peer_u, peer_v):
    a = {k: np.asarray(v) for k, v in locals().items()}
    fox = FOX_HEADS * HD
    w = a["ab_w_in"][0]
    cut = 3 * fox + FOX_HEADS
    w_c = a["c_w_in"][0]
    w_c_q = w_c[:, :SWA_HEADS * HD].reshape(D, SWA_HEADS, HD)[:, SWA_ORDER].reshape(D, SWA_HEADS * HD)
    gains = np.stack([a["norm_mix"][0], a["norm_ffn"][0], a["norm_mix"][1], a["norm_ffn"][1]])
    return [
        ("x", a["x"].reshape(T, D)),
        ("gains", gains.reshape(2 * DEPTH, C, P).transpose(2, 0, 1)),
        ("gain_final", a["norm_final"]),
        ("consts", float_constants()),
        ("masks", mask_constants()),
        ("w_ab", np.concatenate([by_blocks(w[:, :2 * fox]), by_row_chunks(w[:, 2 * fox:3 * fox]), by_row_chunks(w[:, cut:])])),
        ("w_f", w[:, 3 * fox:cut].reshape(C, P, FOX_HEADS).transpose(1, 0, 2)),
        ("f_bias", a["ab_f_bias"].reshape(FOX_HEADS, 1)),
        ("lam_vecs", a["ab_lambda"][0]),
        ("subln", a["ab_subln"][0]),
        ("w_ab_out", by_row_chunks(a["ab_w_out"][0])),
        ("w_c", by_row_chunks(np.concatenate([w_c_q, w_c[:, SWA_HEADS * HD:]], axis=1))),
        ("sinks", a["c_sinks"][0]),
        ("w_c_out", by_row_chunks(a["c_w_out"][0])),
        ("w_pq", np.stack([by_blocks(a["peer_w_q"][l]) for l in range(DEPTH)])),
        ("keys_t", a["peer_sub_keys"].reshape(DEPTH, HC, KEYS, P).transpose(0, 3, 1, 2)),
        ("u_t", a["peer_u"].reshape(DEPTH, KEYS, KEYS, C, P).transpose(0, 1, 4, 3, 2).reshape(DEPTH, KEYS, P, D)),
        ("v_e", a["peer_v"].reshape(DEPTH, KEYS, P, D)),
    ]


def kernel(**inputs):
    import concourse.bacc as bacc
    from concourse.bass_utils import run_bass_kernel_spmd

    nc = bacc.Bacc("TRN2", target_bir_lowering=False, num_devices=1)
    arrays, args = {}, []
    for name, a in laid_out(**inputs):
        a = np.ascontiguousarray(a)
        arrays[f"in_{name}"] = a
        args.append(nc.dram_tensor(f"in_{name}", a.shape, mybir.dt.from_np(a.dtype), kind="ExternalInput").ap())
    args.append(nc.dram_tensor("out_trunk", (T, D), F32, kind="ExternalOutput").ap())
    trunk(nc, *args)
    r = run_bass_kernel_spmd(nc, [arrays], core_ids=[0])
    return r.results[0]["out_trunk"].reshape(1, T, D)
```
